# Optimizing a Trainium2 kernel written in Bass

```python
import math
import jax, jax.numpy as jnp
from jax import lax
import numpy as np

D_MODEL = 1024
BATCH = 1
SEQ = 256
DEPTH = 2

N_MIXERS = 2
N_POOL_LAYERS = (DEPTH + 1) // 2
N_ATTN_LAYERS = DEPTH // 2
POOL_WINDOWS = (2, 4, 8, 16)
N_POOL_GROUPS = len(POOL_WINDOWS)
POOL_GROUP_DIM = D_MODEL // N_POOL_GROUPS
HEAD_DIM = 64
N_Q_HEADS = D_MODEL // HEAD_DIM
N_KV_HEADS = 4
GQA_GROUP = N_Q_HEADS // N_KV_HEADS
WINDOW = 128
BLOCK = 128
ROPE_THETA = 500000.0
ROT_DIM = HEAD_DIM // 4
D_FF = 2816
LN_EPS = 1e-5
DEEPNORM_ALPHA = (2 * DEPTH) ** 0.25
DEEPNORM_BETA = (8 * DEPTH) ** -0.25
NEG_INF = -1e30

kernel_name = "hybrid_pool_swa_sink_macaron_deepnorm"

def layer_norm(x, g, b):
    xf = x.astype(jnp.float32)
    mu = jnp.mean(xf, axis=-1, keepdims=True)
    xc = xf - mu
    var = jnp.mean(xc * xc, axis=-1, keepdims=True)
    y = xc * lax.rsqrt(var + LN_EPS) * g.astype(jnp.float32) + b.astype(jnp.float32)
    return y.astype(x.dtype)

def post_norm(x, sub, g, b):
    return layer_norm(DEEPNORM_ALPHA * x + sub, g, b)

def swiglu(x, w_gate, w_up, w_down):
    h = jax.nn.silu(x @ w_gate) * (x @ w_up)
    return h @ w_down

def pool_mixer(x, w, b, scale):
    B, S, D = x.shape
    xf = x.astype(jnp.float32)
    cs = jnp.pad(jnp.cumsum(xf, axis=1), ((0, 0), (1, 0), (0, 0)))
    csg = cs.reshape(B, S + 1, N_POOL_GROUPS, POOL_GROUP_DIM)
    t = jnp.arange(S)
    means = []
    for g, win in enumerate(POOL_WINDOWS):
        lo = jnp.maximum(t + 1 - win, 0)
        cnt = jnp.minimum(t + 1, win).astype(jnp.float32)
        seg = csg[:, 1:, g] - csg[:, lo, g]
        means.append(seg / cnt[None, :, None])
    pooled = jnp.stack(means, axis=2)
    u = (pooled - xf.reshape(B, S, N_POOL_GROUPS, POOL_GROUP_DIM)).astype(x.dtype)
    y = jnp.einsum('bsgc,gcd->bsgd', u, w).reshape(B, S, D) + b
    return y * scale

def rotary_tables(positions):
    inv_freq = ROPE_THETA ** (-jnp.arange(0, ROT_DIM, 2, dtype=jnp.float32) / ROT_DIM)
    ang = positions.astype(jnp.float32)[..., None] * inv_freq
    return jnp.cos(ang)[:, :, None, :], jnp.sin(ang)[:, :, None, :]

def apply_partial_rotary(t, cos, sin):
    tf = t.astype(jnp.float32)
    half = ROT_DIM // 2
    t1 = tf[..., :half]
    t2 = tf[..., half:ROT_DIM]
    rot = jnp.concatenate([t1 * cos - t2 * sin, t2 * cos + t1 * sin], axis=-1)
    return jnp.concatenate([rot, tf[..., ROT_DIM:]], axis=-1).astype(t.dtype)

def swa_sink_attention(x, cos, sin, w_qkv, b_qkv, sinks, w_o, b_o):
    B, S, D = x.shape
    nb = S // BLOCK
    qkv = x @ w_qkv + b_qkv
    q, k, v = jnp.split(qkv, [N_Q_HEADS * HEAD_DIM, (N_Q_HEADS + N_KV_HEADS) * HEAD_DIM], axis=-1)
    q = apply_partial_rotary(q.reshape(B, S, N_Q_HEADS, HEAD_DIM), cos, sin)
    k = apply_partial_rotary(k.reshape(B, S, N_KV_HEADS, HEAD_DIM), cos, sin)
    v = v.reshape(B, S, N_KV_HEADS, HEAD_DIM)
    q = q.reshape(B, nb, BLOCK, N_KV_HEADS, GQA_GROUP, HEAD_DIM)

    def band(t):
        t = t.reshape(B, nb, BLOCK, N_KV_HEADS, HEAD_DIM)
        prev = jnp.pad(t[:, :-1], ((0, 0), (1, 0), (0, 0), (0, 0), (0, 0)))
        return jnp.concatenate([prev, t], axis=2)

    kb, vb = band(k), band(v)
    s = jnp.einsum('bnqkgd,bnskd->bkgnqs', q, kb).astype(jnp.float32) * (HEAD_DIM ** -0.5)
    qi = jnp.arange(BLOCK)[:, None] + BLOCK
    kj = jnp.arange(2 * BLOCK)[None, :]
    diff = qi - kj
    in_win = (diff >= 0) & (diff < WINDOW)
    key_pos = jnp.arange(nb)[:, None, None] * BLOCK - BLOCK + kj[None]
    valid = in_win[None] & (key_pos >= 0)
    s = jnp.where(valid, s, NEG_INF)
    sink = sinks.astype(jnp.float32).reshape(N_KV_HEADS, GQA_GROUP)[None, :, :, None, None, None]
    m = jnp.maximum(jnp.max(s, axis=-1, keepdims=True), sink)
    p = jnp.exp(s - m)
    denom = jnp.sum(p, axis=-1, keepdims=True) + jnp.exp(sink - m)
    p = (p / denom).astype(x.dtype)
    o = jnp.einsum('bkgnqs,bnskd->bnqkgd', p, vb).reshape(B, S, N_Q_HEADS * HEAD_DIM)
    return o @ w_o + b_o

def setup_inputs(seed: int = 0) -> dict:
    key = jax.random.key(seed)
    ks = jax.random.split(key, 16)
    f32 = jnp.float32
    D, F = D_MODEL, D_FF
    QKV = (N_Q_HEADS + 2 * N_KV_HEADS) * HEAD_DIM
    x = jax.random.normal(ks[0], (BATCH, SEQ, D), f32)
    offs = jax.random.randint(ks[1], (BATCH, 1), 0, 1024, dtype=jnp.int32)
    positions = jnp.arange(SEQ, dtype=jnp.int32)[None, :] + offs
    ln_g = 1.0 + 0.02 * jax.random.normal(ks[2], (DEPTH, 3, D), f32)
    ln_b = 0.02 * jax.random.normal(ks[3], (DEPTH, 3, D), f32)
    ffn_w_gate = jax.random.normal(ks[4], (DEPTH, 2, D, F), f32) * D ** -0.5
    ffn_w_up = jax.random.normal(ks[5], (DEPTH, 2, D, F), f32) * D ** -0.5
    ffn_w_down = jax.random.normal(ks[6], (DEPTH, 2, F, D), f32) * (F ** -0.5 * DEEPNORM_BETA)
    pool_w = jax.random.normal(ks[7], (N_POOL_LAYERS, N_POOL_GROUPS, POOL_GROUP_DIM, POOL_GROUP_DIM), f32) * (POOL_GROUP_DIM ** -0.5 * DEEPNORM_BETA)
    pool_b = 0.01 * jax.random.normal(ks[8], (N_POOL_LAYERS, D), f32)
    pool_scale = 1.0 + 0.1 * jax.random.normal(ks[9], (N_POOL_LAYERS, D), f32)
    attn_w_qkv = jax.random.normal(ks[10], (N_ATTN_LAYERS, D, QKV), f32) * D ** -0.5
    attn_b_qkv = 0.01 * jax.random.normal(ks[11], (N_ATTN_LAYERS, QKV), f32)
    attn_sinks = 0.5 * jax.random.normal(ks[12], (N_ATTN_LAYERS, N_Q_HEADS), f32)
    attn_w_o = jax.random.normal(ks[13], (N_ATTN_LAYERS, N_Q_HEADS * HEAD_DIM, D), f32) * ((N_Q_HEADS * HEAD_DIM) ** -0.5 * DEEPNORM_BETA)
    attn_b_o = 0.01 * jax.random.normal(ks[14], (N_ATTN_LAYERS, D), f32)
    return {"x": x, "positions": positions, "ln_g": ln_g, "ln_b": ln_b,
            "ffn_w_gate": ffn_w_gate, "ffn_w_up": ffn_w_up, "ffn_w_down": ffn_w_down,
            "pool_w": pool_w, "pool_b": pool_b, "pool_scale": pool_scale,
            "attn_w_qkv": attn_w_qkv, "attn_b_qkv": attn_b_qkv, "attn_sinks": attn_sinks,
            "attn_w_o": attn_w_o, "attn_b_o": attn_b_o}

def reference(x, positions, ln_g, ln_b, ffn_w_gate, ffn_w_up, ffn_w_down,
              pool_w, pool_b, pool_scale,
              attn_w_qkv, attn_b_qkv, attn_sinks, attn_w_o, attn_b_o):
    cos, sin = rotary_tables(positions)
    for i in range(DEPTH):
        x = post_norm(x, 0.5 * swiglu(x, ffn_w_gate[i, 0], ffn_w_up[i, 0], ffn_w_down[i, 0]), ln_g[i, 0], ln_b[i, 0])
        j = i // N_MIXERS
        if i % N_MIXERS == 0:
            mix = pool_mixer(x, pool_w[j], pool_b[j], pool_scale[j])
        else:
            mix = swa_sink_attention(x, cos, sin, attn_w_qkv[j], attn_b_qkv[j], attn_sinks[j], attn_w_o[j], attn_b_o[j])
        x = post_norm(x, mix, ln_g[i, 1], ln_b[i, 1])
        x = post_norm(x, 0.5 * swiglu(x, ffn_w_gate[i, 1], ffn_w_up[i, 1], ffn_w_down[i, 1]), ln_g[i, 2], ln_b[i, 2])
    return x


_drawn_inputs = setup_inputs


def setup_inputs(seed=0):
    import zlib

    import numpy as np

    out = dict(_drawn_inputs(seed))
    spreads = {}
    factors = {'pool_b': 8.0, 'attn_b_qkv': 8.0, 'attn_sinks': 8.0, 'attn_b_o': 8.0}
    for name, (base, spread) in spreads.items():
        noise = np.random.default_rng([zlib.crc32(name.encode()), seed]).standard_normal(out[name].shape)
        drawn = base * np.exp(spread * noise) if base else spread * noise
        out[name] = __import__('jax').numpy.asarray(drawn.astype(out[name].dtype))
    for name, factor in factors.items():
        out[name] = (out[name] * factor).astype(out[name].dtype)
    return out
```

```python
import math
from contextlib import ExitStack

import numpy as np

import concourse.bass as bass
from concourse import mybir

P = 128
D = 1024
S = 256
F = 2816
KT = D // P
TT = S // P
UNITS = F // P
FFNS = 4
HD = 64
NQ = 16
NKV = 4
ROT = 16
HALF = ROT // 2
THETA = 500000.0
WINDOWS = (2, 4, 8, 16)
GC = D // len(WINDOWS)
ALPHA = 4.0 ** 0.25
EPS = 1e-5
SCALE = HD ** -0.5
NEG = -1e30
LAST = 3

QKV_UNITS = 6
POOL_UNITS = 2
WO_UNITS = 8
G0 = [0, UNITS, 2 * UNITS, 3 * UNITS + QKV_UNITS]
D0 = [0, UNITS + POOL_UNITS, 2 * UNITS + POOL_UNITS, 3 * UNITS + POOL_UNITS + WO_UNITS]
G_QKV = 3 * UNITS
D_POOL = UNITS
D_WO = 3 * UNITS + POOL_UNITS
G_SLOTS = 2
D_SLOTS = 4

T_EVENT = {1: 1, 2: 2, 3: 3, 4: 4}
FFN_NORM = [0, 2, 3, 5]
FFN_EVENT = [0, 1, 2, 4]
QKV_EVENT = 3


def trunk_kernel(nc, x, positions, ln_g, ln_b, w_gate, w_up, w_down, pool_w, pool_b, pool_scale,
                 w_qkv, b_qkv, sinks, w_o, b_o, bands, masks, out):
    f32 = mybir.dt.float32
    f32r = mybir.dt.float32r
    i32 = mybir.dt.int32
    ALU = mybir.AluOpType
    ACT = mybir.ActivationFunctionType
    AX = mybir.AxisListType

    with ExitStack() as ctx:
        def sb(name, shape, dt=f32):
            return ctx.enter_context(nc.sbuf_tensor(name, shape, dt))

        def sem(name):
            return ctx.enter_context(nc.semaphore(name))

        raw_g = sb("raw_g", [P, 2, 2, 2048])
        raw_d = sb("raw_d", [P, 2, 2, 1024])
        g_hi = sb("g_hi", [P, G_SLOTS, 2048], f32r)
        g_lo = sb("g_lo", [P, G_SLOTS, 2048], f32r)
        d_hi = sb("d_hi", [P, D_SLOTS, 1024], f32r)
        d_lo = sb("d_lo", [P, D_SLOTS, 1024], f32r)
        xT_hi = sb("xT_hi", [P, KT, S], f32r)
        xT_lo = sb("xT_lo", [P, KT, S], f32r)
        hT_hi = sb("hT_hi", [P, D_SLOTS, S], f32r)
        hT_lo = sb("hT_lo", [P, D_SLOTS, S], f32r)
        xn = sb("xn", [P, TT, D])
        ax = sb("ax", [P, TT, D])
        xf = sb("xf", [P, KT, P])
        silu = sb("silu", [P, 2, S])
        hf = sb("hf", [P, 2, S])
        gb = sb("gb", [P, 2, D])
        aux = sb("aux", [P, 2560])
        cst = sb("cst", [P, 4, P])
        lnT = sb("lnT", [P, 2, 6, KT])
        lnrow = sb("lnrow", [6 * KT, 2, P])
        stats = sb("stats", [P, 2, 6])
        mv = sb("mv", [P, 2, 2])
        rstd = sb("rstd", [P, 2, 2])
        mhalf = sb("mhalf", [P, 1])
        pos_i = sb("pos_i", [P, TT], i32)
        ang = sb("ang", [P, 8, TT, HALF])
        invf = sb("invf", [P, HALF])
        rot = sb("rot", [P, TT, 3, HALF])
        sinkb = sb("sinkb", [P, NQ])
        sm = sb("sm", [P, 2, 6, 4])
        vd = sb("vd", [P, TT, NKV, 2, HD])
        qT = sb("qT", [P, KT, S])
        kT = sb("kT", [P, NKV, 2, S])
        band = qT[:, :, :].rearrange("p k s -> p (k s)")[:, 0:4 * 272].rearrange("p (g c) -> p g c", g=4)
        kd = xf[:, :, :].rearrange("p k s -> p (k s)").rearrange("p (t g e d) -> p t g e d", t=TT, g=NKV, e=2)
        sc = [silu[:, :, :].rearrange("p a s -> p (a s)").rearrange("p (h j) -> p h j", h=4),
              hf[:, :, :].rearrange("p a s -> p (a s)").rearrange("p (h j) -> p h j", h=4)]
        pT = [gb[:, i, :].rearrange("p (b h q) -> p b h q", b=2, h=4) for i in range(2)]

        ps = ctx.enter_context(nc.psum_tensor("ps", [P, 8, 512], f32))
        ACC = [[ps[:, 2 * t + h, :] for h in range(2)] for t in range(TT)]
        WORK = 4

        g_in = [sem("g_in0"), sem("g_in1")]
        d_in = [sem("d_in0"), sem("d_in1")]
        g_hi_done = sem("g_hi_done")
        g_lo_done = sem("g_lo_done")
        d_hi_done = sem("d_hi_done")
        d_lo_done = sem("d_lo_done")
        d_scaled = sem("d_scaled")
        g_used = sem("g_used")
        d_used = sem("d_used")
        silu_done = sem("silu_done")
        hf_done = sem("hf_done")
        h_hi_done = sem("h_hi_done")
        h_lo_done = sem("h_lo_done")
        acc_done = sem("acc_done")
        stat_done = sem("stat_done")
        var_done = sem("var_done")
        rstd_done = sem("rstd_done")
        xn_done = sem("xn_done")
        tr_done = sem("tr_done")
        xf_done = sem("xf_done")
        x_hi_done = sem("x_hi_done")
        x_lo_done = sem("x_lo_done")
        ax_done = sem("ax_done")
        u_done = sem("u_done")
        u_hi_done = sem("u_hi_done")
        u_lo_done = sem("u_lo_done")
        axb_done = sem("axb_done")
        bs_done = sem("bs_done")
        x_in = sem("x_in")
        small_in = sem("small_in")
        band_in = sem("band_in")
        gb_in = sem("gb_in")
        aux_in = sem("aux_in")
        cst_in = sem("cst_in")
        consts = sem("consts")
        lnT_ps = sem("lnT_ps")
        lnT_done = sem("lnT_done")
        kz_done = sem("kz_done")
        ang_done = sem("ang_done")
        sin_done = sem("sin_done")
        order = sem("dve_order")
        qkv_done = sem("qkv_done")
        qkv_sb = sem("qkv_sb")
        dup_done = sem("dup_done")
        qkT_ps = sem("qkT_ps")
        qkT_done = sem("qkT_done")
        s_done = sem("s_done")
        diag_done = sem("diag_done")
        s_sb = sem("s_sb")
        m_done = sem("m_done")
        e_done = sem("e_done")
        p_done = sem("p_done")
        pT_ps = sem("pT_ps")
        pT_a = sem("pT_a")
        pT_v = sem("pT_v")
        oT_ps = sem("oT_ps")
        oT_hi_done = sem("oT_hi_done")
        oT_lo_done = sem("oT_lo_done")
        y_done = sem("y_done")
        out_done = sem("out_done")

        TASKS = [(g, n) for g in range(NKV) for n in range(TT)]

        def after(eng, s, value):
            if not isinstance(value, int) or value > 0:
                eng.wait_ge(s, value)

        def raw_unit(G, half):
            c = raw_g[:, (G // 2) % 2, half, :].rearrange("p (k f) -> p k f", k=KT)
            return c[:, :, (G % 2) * P:(G % 2 + 1) * P]

        def raw_qkv(G, half):
            return raw_g[:, (G // 2) % 2, G % 2, half * 1024:(half + 1) * 1024].rearrange("p (k f) -> p k f", k=KT)

        def g_half(buf, G, half):
            return buf[:, G % G_SLOTS, half * 1024:(half + 1) * 1024].rearrange("p (k f) -> p k f", k=KT)

        two_banks = ps[:, WORK:WORK + 2, :].rearrange("p b (h j) -> p (b h) j", h=2)
        rtmp = sb("rtmp", [P, 2, 8, ROT])
        prevT = sb("prevT", [P, 1, P])

        block = ctx.enter_context(nc.Block())

        @block.sync
        def _(sp):
            gate_v = w_gate.rearrange("l i (k p) f -> (l i) p k f", p=P)
            up_v = w_up.rearrange("l i (k p) f -> (l i) p k f", p=P)
            down_v = w_down.rearrange("l i (u p) d -> (l i) p u d", p=P)
            qkv_v = w_qkv[0].rearrange("(k p) c -> p k c", p=P)
            wo_v = w_o[0].rearrange("(u p) d -> p u d", p=P)
            pool_v = pool_w[0].rearrange("g (k p) d -> p k g d", p=P)

            def load_ffn(f, c, it):
                C, E = G0[f] // 2 + c, D0[f] // 2 + c
                after(sp, g_lo_done, 4 * (C - 1) + 8 * it)
                dst = raw_g[:, C % 2, :, :].rearrange("p m (k f) -> p m k f", k=KT)
                for m, w in enumerate((gate_v, up_v)):
                    sp.dma_start(dst[:, m], w[f, :, :, bass.ds(2 * P * c + 4 * P * it, 2 * P)]).then_inc(g_in[C % 2], 16)
                after(sp, d_lo_done, 2 * (E - 1) + 4 * it)
                for m in range(2):
                    sp.dma_start(raw_d[:, E % 2, m, :], down_v[f, :, bass.ds(2 * c + m + 4 * it, 1), :].rearrange("p a d -> p (a d)")).then_inc(d_in[E % 2], 16)

            def load_d(E, srcs):
                after(sp, d_lo_done, 2 * (E - 1))
                for m, src in enumerate(srcs):
                    dst = raw_d[:, E % 2, m, :]
                    sp.dma_start(dst.rearrange("p (g d) -> p g d", g=4) if len(src.shape) == 3 else dst, src).then_inc(d_in[E % 2], 16)

            sp.dma_start(xn[:, :, :], x[0].rearrange("(t p) d -> p t d", p=P)).then_inc(x_in, 16)
            for f in range(FFNS):
                if f == 0:
                    for c in range(2):
                        load_ffn(f, c, 0)
                first = 2 if f == 0 else 0
                with sp.Fori(0, (UNITS // 2 - 1 - first) // 2) as it:
                    for c in range(2):
                        load_ffn(f, first + c, it)
                load_ffn(f, UNITS // 2 - 1, 0)
                if f == 0:
                    load_d(D_POOL // 2, [pool_v[:, k] for k in range(2)])
                if f == 2:
                    for i, j in enumerate((2, 0, 1)):
                        C = G_QKV // 2 + i
                        after(sp, g_lo_done, 4 * (C - 1))
                        for m in range(2):
                            sp.dma_start(raw_g[:, C % 2, m, :].rearrange("p (k c) -> p k c", k=4),
                                         qkv_v[:, 4 * m:4 * m + 4, 512 * j:512 * (j + 1)]).then_inc(g_in[C % 2], 16)
                        if i < 2:
                            load_d(D_WO // 2 + i, [wo_v[:, 2 * i + m] for m in range(2)])
                    for i in range(2, 4):
                        load_d(D_WO // 2 + i, [wo_v[:, 2 * i + m] for m in range(2)])
            for t in range(TT):
                for h in range(2):
                    sp.wait_ge(y_done, 2 * t + h + 1)
                    sp.dma_start(out[0, t * P:(t + 1) * P, 512 * h:512 * (h + 1)], xn[:, t, 512 * h:512 * (h + 1)]).then_inc(out_done, 16)
            sp.wait_ge(out_done, 64)

        @block.gpsimd
        def _(gp):
            gp.dma_start(cst[:, :, :], masks.rearrange("m p q -> p m q")).then_inc(cst_in, 16)
            gp.dma_start(lnrow[:, 0, :], ln_g.rearrange("l n (k p) -> (l n k) p", p=P)).then_inc(small_in, 16)
            gp.dma_start(lnrow[:, 1, :], ln_b.rearrange("l n (k p) -> (l n k) p", p=P)).then_inc(small_in, 16)
            gp.dma_start(pos_i[:, :], positions[0].rearrange("(t p) -> p t", p=P), allow_slow_non_contiguous=True).then_inc(small_in, 16)
            gp.dma_start(sinkb[:, :], sinks[0:1, :].to_broadcast([P, NQ])).then_inc(small_in, 16)
            gp.dma_start(band[:, :, :], bands.rearrange("g p c -> p g c")).then_inc(band_in, 16)
            for j in range(HALF):
                gp.memset(invf[:, j:j + 1], float(np.float32(THETA) ** np.float32(-2.0 * j / ROT)))
            gp.memset(mhalf[:, :], -0.5).then_inc(consts, 1)
            gp.memset(kT[:, :, :, :], 0.0).then_inc(kz_done, 1)
            gp.dma_start(aux[:, 0:D], pool_scale[0:1, :].to_broadcast([P, D])).then_inc(aux_in, 16)
            gp.dma_start(aux[:, D:2 * D], pool_b[0:1, :].to_broadcast([P, D])).then_inc(aux_in, 16)
            gp.wait_ge(aux_in, 32)
            gp.tensor_tensor(aux[:, D:2 * D], aux[:, D:2 * D], aux[:, 0:D], ALU.mult).then_inc(bs_done, 1)

            for n in range(6):
                if n > 0:
                    gp.wait_ge(ax_done, 2 * n + 2)
                if n == 4:
                    gp.wait_ge(oT_ps, len(TASKS))
                gp.dma_start(gb[:, 0, :], ln_g[n // 3, n % 3:n % 3 + 1, :].to_broadcast([P, D])).then_inc(gb_in, 16)
                gp.dma_start(gb[:, 1, :], ln_b[n // 3, n % 3:n % 3 + 1, :].to_broadcast([P, D])).then_inc(gb_in, 16)
                for t in range(TT):
                    gp.wait_ge(stat_done, 2 * n + t + 1)
                    gp.tensor_scalar(rstd[:, t, 0:1], mv[:, t, 1:2], EPS, None, ALU.add).then_inc(var_done, 1)
                    gp.wait_ge(var_done, 2 * n + t + 1)
                    gp.tensor_tensor(rstd[:, t, 1:2], rstd[:, t, 0:1], mhalf[:, :], ALU.pow).then_inc(rstd_done, 1)
                if n == 0:
                    gp.wait_ge(bs_done, 1)
                    gp.wait_ge(u_done, KT // 2)
                    for t in range(TT):
                        gp.wait_ge(ax_done, 2 * (n + 1) + t + 1)
                        gp.tensor_tensor(ax[:, t, :], ax[:, t, :], aux[:, D:2 * D], ALU.add).then_inc(axb_done, 1)
                if n == 1:
                    gp.wait_ge(d_scaled, 2)
                    gp.wait_ge(axb_done, 2)
                    gp.dma_start(aux[:, 0:1536], b_qkv[0:1, :].to_broadcast([P, 1536])).then_inc(aux_in, 16)
                    gp.dma_start(aux[:, 1536:2560], b_o[0:1, :].to_broadcast([P, D])).then_inc(aux_in, 16)
                if n == 3:
                    gp.wait_ge(aux_in, 64)
                    for t in range(TT):
                        gp.wait_ge(ax_done, 2 * (n + 1) + t + 1)
                        gp.tensor_tensor(ax[:, t, :], ax[:, t, :], aux[:, 1536:2560], ALU.add).then_inc(axb_done, 1)

        def attention_act(act, g_split, d_split):
            def wo_split(k):
                d_split(D_WO + k)

            def transposed(chunk):
                for t in range(TT):
                    act.wait_ge(qkT_ps, 2 * chunk + t + 1)
                    bank = ps[:, WORK + 2 + t, :].rearrange("p (a s) -> p a s", a=4)
                    if chunk == 0:
                        if t == 0:
                            act.wait_ge(kz_done, 1)
                        act.activation(kT[0:HD, :, 0, t * P:(t + 1) * P], bank[0:HD], ACT.Copy)
                        act.activation(kT[HD:P, :, 1, t * P:(t + 1) * P], bank[HD:P], ACT.Copy).then_inc(qkT_done, 1)
                    else:
                        act.activation(qT[:, 4 * chunk - 4:4 * chunk, t * P:(t + 1) * P], bank, ACT.Copy).then_inc(qkT_done, 1)

            def diag(i):
                g, n = TASKS[i]
                if n == 1:
                    act.wait_ge(s_done, i + 1)
                    after(act, pT_ps, i - 1)
                    act.activation(sc[i % 2][:, :, :], two_banks[:, :, P:2 * P], ACT.Copy).then_inc(diag_done, 1)

            def exps(i):
                act.wait_ge(m_done, i + 1)
                for h in range(4):
                    act.activation(sc[i % 2][:, h, :], sc[i % 2][:, h, :], ACT.Exp, bias=sm[:, i % 2, 1, h:h + 1],
                                   scale=SCALE, accum_out=sm[:, i % 2, 3, h:h + 1])
                act.activation(sm[:, i % 2, 4, :], sm[:, i % 2, 2, :], ACT.Exp).then_inc(e_done, 1)

            def pT_copy(i):
                if TASKS[i][1] == 0:
                    act.wait_ge(pT_ps, i + 1)
                    act.activation(pT[i % 2][:, 1], ps[:, WORK + 2, :].rearrange("p (h q) -> p h q", h=4), ACT.Copy).then_inc(pT_a, 1)

            def o_hi(i):
                g, n = TASKS[i]
                act.wait_ge(oT_ps, i + 1)
                bank = ps[:, WORK + 3, :].rearrange("p (a e q) -> p a e q", a=2, e=2)
                act.activation(xT_hi[0:HD, 2 * g:2 * g + 2, n * P:(n + 1) * P], bank[0:HD, :, 0, :], ACT.Copy)
                act.activation(xT_hi[HD:P, 2 * g:2 * g + 2, n * P:(n + 1) * P], bank[HD:P, :, 1, :], ACT.Copy).then_inc(oT_hi_done, 1)

            act.wait_ge(qkv_sb, 1)
            act.activation(kd[:, :, :, 1, :], kd[:, :, :, 0, :], ACT.Copy)
            act.activation(vd[:, :, :, 1, :], vd[:, :, :, 0, :], ACT.Copy).then_inc(dup_done, 1)
            for G in range(G_QKV + 2, G_QKV + 4):
                g_split(G, src=raw_qkv)
            wo_split(0)
            wo_split(1)
            transposed(0)
            for G in range(G_QKV + 4, G_QKV + 6):
                g_split(G, src=raw_qkv)
            transposed(1)
            wo_split(2)
            wo_split(3)
            exps(0)
            for i in range(len(TASKS)):
                if i == 1:
                    transposed(2)
                if i + 1 < len(TASKS):
                    diag(i + 1)
                pT_copy(i)
                if i + 1 < len(TASKS):
                    exps(i + 1)
                o_hi(i)
                if i >= 4:
                    wo_split(i)
            for G in range(G0[3], G0[3] + 2):
                g_split(G)


        @block.scalar
        def _(act):
            def g_split(G, it=0, src=raw_unit):
                act.wait_ge(g_in[(G // 2) % 2], 32 * (G // 4 + 1) + 32 * it)
                after(act, g_used, G - G_SLOTS + 1 + 4 * it)
                for half in range(2):
                    act.activation(g_half(g_hi, G, half), src(G, half), ACT.Copy).then_inc(g_hi_done, 1)

            def d_split(E, it=0):
                act.wait_ge(d_in[(E // 2) % 2], 32 * (E // 4 + 1) + 32 * it)
                after(act, d_used, E - D_SLOTS + 1 + 4 * it)
                act.activation(d_hi[:, E % D_SLOTS, :], raw_d[:, (E // 2) % 2, E % 2, :], ACT.Copy).then_inc(d_hi_done, 1)

            def silu_of(f, u, it=0):
                act.wait_ge(g_used, G0[f] + u + 1 + 4 * it)
                act.activation(silu[:, u % 2, :], ps[:, WORK + u % 2, 0:S], ACT.Silu).then_inc(silu_done, 1)

            def h_hi_of(f, u, it=0):
                act.wait_ge(hf_done, UNITS * f + u + 1 + 4 * it)
                act.activation(hT_hi[:, (D0[f] + u) % D_SLOTS, :], hf[:, u % 2, :], ACT.Copy).then_inc(h_hi_done, 1)

            def unit(f, u, it=0):
                silu_of(f, u, it)
                if u + 2 < UNITS or f != 3:
                    src = raw_qkv if f == 2 and u + 2 >= UNITS else raw_unit
                    h_first = u + 2 >= UNITS
                    if h_first:
                        h_hi_of(f, u, it)
                    g_split(G0[f] + u + 2, it, src)
                    if not h_first:
                        h_hi_of(f, u, it)
                else:
                    h_hi_of(f, u, it)
                if u + 2 < UNITS:
                    d_split(D0[f] + u + 2, it)

            def x_hi(e, tiles=range(TT)):
                for t in tiles:
                    for q in range(2):
                        act.wait_ge(xf_done, 4 * e + 2 * t + q + 1)
                        act.activation(xT_hi[:, 4 * q:4 * q + 4, t * P:(t + 1) * P], xf[:, 4 * q:4 * q + 4, :], ACT.Copy).then_inc(x_hi_done, 1)

            act.wait_ge(ang_done, 1)
            act.activation(rot[:, :, 1, :], ang[:, 0], ACT.Sin)
            act.activation(rot[:, :, 0, :], ang[:, 1], ACT.Sin).then_inc(sin_done, 1)
            for t in range(TT):
                x_hi(0, (t,))
                g_split(t)
            for f in range(FFNS):
                for u in range(2):
                    d_split(D0[f] + u)
                if f == 0:
                    for u in range(4):
                        unit(f, u)
                first = 4 if f == 0 else 0
                with act.Fori(0, (UNITS - 2 - first) // 4) as it:
                    for u in range(first, first + 4):
                        unit(f, u, it)
                for u in range(UNITS - 2, UNITS):
                    unit(f, u)
                if f == 0:
                    for c in range(KT // 2):
                        act.wait_ge(u_done, c + 1)
                        act.activation(xT_hi[:, 2 * c:2 * c + 2, :], ps[:, WORK + c, :].rearrange("p (a s) -> p a s", a=2), ACT.Copy).then_inc(u_hi_done, 1)
                    for k in range(POOL_UNITS):
                        act.wait_ge(d_scaled, k + 1)
                        d_split(D_POOL + k)
                    x_hi(1)
                if f == 1:
                    x_hi(2)
                if f == 2:
                    x_hi(QKV_EVENT)
                    attention_act(act, g_split, d_split)
                    x_hi(4)

        def rotary_tables(dve, link):
            dve.wait_ge(small_in, 64)
            dve.wait_ge(consts, 1)
            turn, parts = 2.0 * math.pi, []
            for i in range(4):
                grid = 2.0 ** (9 + 11 * i)
                part = math.floor(turn * grid) / grid if i < 3 else float(np.float32(turn))
                parts.append(part)
                turn -= part
            A = [ang[:, i] for i in range(8)]
            magic = 1.5 * 2.0 ** 23
            link(dve.tensor_copy(ang[:, 7, :, 0], pos_i[:, :]))
            link(dve.tensor_tensor(A[0], ang[:, 7, :, 0:1].to_broadcast([P, TT, HALF]),
                                   invf[:, :].rearrange("p (a j) -> p a j", a=1).to_broadcast([P, TT, HALF]), ALU.mult))
            link(dve.tensor_scalar(A[2], A[0], 1.0 / (2.0 * math.pi), magic, ALU.mult, ALU.add))
            link(dve.tensor_scalar(A[2], A[2], magic, None, ALU.subtract))
            link(dve.tensor_scalar(A[3], A[2], 1.0 / 2048, magic, ALU.mult, ALU.add))
            link(dve.tensor_scalar(A[3], A[3], magic, 2048.0, ALU.subtract, ALU.mult))
            link(dve.tensor_tensor(A[2], A[2], A[3], ALU.subtract))
            for part in parts:
                for digit in (A[3], A[2]):
                    link(dve.scalar_tensor_tensor(A[0], digit, -part, A[0], ALU.mult, ALU.add))
            link(dve.tensor_scalar(A[1], A[0], math.pi / 2, None, ALU.add))
            link(dve.tensor_scalar(A[4], A[1], math.pi, -2.0 * math.pi, ALU.is_gt, ALU.mult))
            link(dve.tensor_tensor(A[1], A[1], A[4], ALU.add))
            top = 3.1415925
            link(dve.tensor_scalar(A[0], A[0], top, -top, ALU.min, ALU.max))
            dve.tensor_scalar(A[1], A[1], top, -top, ALU.min, ALU.max).then_inc(ang_done, 1)
            dve.wait_ge(sin_done, 1)
            link(dve.tensor_scalar(rot[:, :, 2, :], rot[:, :, 1, :], -1.0, None, ALU.mult))

        def attention_dve(dve, link, note, g_split, d_split):
            def rotate(v, tmp_a, tmp_b, heads, t):
                cos, sin, nsin = (rot[:, t, c, :].rearrange("p (a j) -> p a j", a=1).to_broadcast([P, heads, HALF]) for c in range(3))
                lo, hi = v[:, :, 0:HALF], v[:, :, HALF:ROT]
                dve.tensor_tensor(tmp_a[:, :, 0:HALF], lo, cos, ALU.mult)
                dve.tensor_tensor(tmp_a[:, :, HALF:ROT], hi, cos, ALU.mult)
                dve.tensor_tensor(tmp_b[:, :, 0:HALF], hi, nsin, ALU.mult)
                link(dve.tensor_tensor(tmp_b[:, :, HALF:ROT], lo, sin, ALU.mult))
                return dve.tensor_tensor(v[:, :, 0:ROT], tmp_a, tmp_b, ALU.add)

            def chunk(c):
                for t in range(TT):
                    dve.wait_ge(qkv_done, 2 * c + t + 1)
                    src = ps[:, (2 * c + t) % 4, :]
                    if c == 0:
                        as_heads = lambda v: v.rearrange("p (g d) -> p g d", g=NKV)
                        dve.tensor_tensor(vd[:, t, :, 0, :], as_heads(src[:, 256:512]), as_heads(aux[:, 1280:1536]), ALU.add)
                        v, heads = kd[:, t, :, 0, :], NKV
                        link(dve.tensor_tensor(v, as_heads(src[:, 0:256]), as_heads(aux[:, 1024:1280]), ALU.add))
                    else:
                        lo = 512 * (c - 1)
                        flat, heads = xn[:, t, lo:lo + 512], 8
                        v = flat.rearrange("p (h d) -> p h d", h=8)
                        link(dve.tensor_tensor(flat, src, aux[:, lo:lo + 512], ALU.add))
                    tmp = rtmp[:, :, 0:heads, :]
                    last = rotate(v, tmp[:, 0], tmp[:, 1], heads, t)
                    if t == 0:
                        link(last)
                last.then_inc(qkv_sb, 1)

            def scores(i):
                g, n = TASKS[i]
                s = sc[i % 2]
                if n == 0:
                    dve.wait_ge(s_done, i + 1)
                    after(dve, pT_ps, i - 1)
                    ins = dve.tensor_tensor(s[:, :, :], ps[:, WORK, :].rearrange("p (h j) -> p h j", h=4),
                                            cst[:, 1:2, :].to_broadcast([P, 4, P]), ALU.add)
                else:
                    dve.wait_ge(diag_done, g + 1)
                    ins = dve.copy_predicated(s[:, :, :], cst[:, 2:3, :].bitcast(i32).to_broadcast([P, 4, P]), two_banks[:, :, 0:P])
                ins.then_inc(s_sb, 1)
                dve.wait_ge(s_sb, i + 1)
                st = sm[:, i % 2]
                sink = sinkb[:, 4 * g:4 * g + 4]
                link(dve.tensor_reduce(st[:, 0, :], s[:, :, :], axis=AX.X, op=ALU.max))
                link(dve.scalar_tensor_tensor(st[:, 5, :], st[:, 0, :], SCALE, sink, ALU.mult, ALU.max))
                dve.tensor_tensor(st[:, 2, :], sink, st[:, 5, :], ALU.subtract)
                dve.tensor_scalar(st[:, 1, :], st[:, 5, :], -1.0, None, ALU.mult).then_inc(m_done, 1)

            def probabilities(i):
                st = sm[:, i % 2]
                dve.wait_ge(e_done, i + 1)
                link(dve.tensor_tensor(st[:, 5, :], st[:, 3, :], st[:, 4, :], ALU.add))
                link(dve.reciprocal(st[:, 0, :], st[:, 5, :]))
                dve.tensor_tensor(sc[i % 2][:, :, :], sc[i % 2][:, :, :], st[:, 0, :].rearrange("p (h a) -> p h a", a=1).to_broadcast([P, 4, P]), ALU.mult).then_inc(p_done, 1)

            def pT_masked(i):
                if TASKS[i][1] == 1:
                    dve.wait_ge(pT_ps, i + 1)
                    src = ps[:, WORK + 2, :].rearrange("p (h q) -> p h q", h=4)
                    dve.tensor_tensor(pT[i % 2][:, 1], src, cst[:, 3:4, :].to_broadcast([P, 4, P]), ALU.mult)
                    dve.tensor_tensor(pT[i % 2][:, 0], src, prevT[:, :, :].to_broadcast([P, 4, P]), ALU.mult).then_inc(pT_v, 1)

            def o_lo(i):
                g, n = TASKS[i]
                dve.wait_ge(oT_hi_done, i + 1)
                bank = ps[:, WORK + 3, :].rearrange("p (a e q) -> p a e q", a=2, e=2)
                for e, rows in enumerate((slice(0, HD), slice(HD, P))):
                    last = dve.tensor_tensor(xT_lo[rows, 2 * g:2 * g + 2, n * P:(n + 1) * P], bank[rows, :, e, :],
                                             xT_hi[rows, 2 * g:2 * g + 2, n * P:(n + 1) * P].bitcast(f32), ALU.subtract)
                last.then_inc(oT_lo_done, 1)

            dve.wait_ge(aux_in, 64)
            link(dve.tensor_scalar(prevT[:, 0, :], cst[:, 3, :], -1.0, 1.0, ALU.mult, ALU.add))
            chunk(0)
            for G in range(G_QKV + 2, G_QKV + 4):
                g_split(G, src=raw_qkv)
            d_split(D_WO)
            d_split(D_WO + 1)
            chunk(1)
            for G in range(G_QKV + 4, G_QKV + 6):
                g_split(G, src=raw_qkv)
            d_split(D_WO + 2)
            d_split(D_WO + 3)
            scores(0)
            for i in range(len(TASKS)):
                probabilities(i)
                if i + 1 < len(TASKS):
                    scores(i + 1)
                pT_masked(i)
                if i == 0:
                    chunk(2)
                o_lo(i)
                if i >= 4:
                    d_split(D_WO + i)
            for G in range(G0[3], G0[3] + 2):
                g_split(G)


        @block.vector
        def _(dve):
            count = [0]

            def note(ins):
                count[0] += 1
                ins.then_inc(order, 1)
                return count[0]

            def link(ins):
                dve.wait_ge(order, note(ins))

            def g_split(G, it=0, src=raw_unit):
                for half in range(2):
                    dve.wait_ge(g_hi_done, 2 * G + half + 1 + 8 * it)
                    dve.tensor_tensor(g_half(g_lo, G, half), src(G, half), g_half(g_hi, G, half).bitcast(f32), ALU.subtract).then_inc(g_lo_done, 1)

            def d_split(E, it=0):
                dve.wait_ge(d_hi_done, E + 1 + 4 * it)
                dve.tensor_tensor(d_lo[:, E % D_SLOTS, :], raw_d[:, (E // 2) % 2, E % 2, :], d_hi[:, E % D_SLOTS, :].bitcast(f32), ALU.subtract).then_inc(d_lo_done, 1)

            def h_of(f, u, it=0):
                dve.wait_ge(silu_done, UNITS * f + u + 1 + 4 * it)
                dve.tensor_tensor(hf[:, u % 2, :], silu[:, u % 2, :], ps[:, WORK + u % 2, S:2 * S], ALU.mult).then_inc(hf_done, 1)

            def h_lo_of(f, u, it=0):
                dve.wait_ge(h_hi_done, UNITS * f + u + 1 + 4 * it)
                slot = (D0[f] + u) % D_SLOTS
                dve.tensor_tensor(hT_lo[:, slot, :], hf[:, u % 2, :], hT_hi[:, slot, :].bitcast(f32), ALU.subtract).then_inc(h_lo_done, 1)

            def unit(f, u, it=0):
                h_of(f, u, it)
                late = u + 2 >= UNITS
                if late:
                    h_lo_of(f, u, it)
                if not late or f != 3:
                    g_split(G0[f] + u + 2, it, raw_qkv if f == 2 and late else raw_unit)
                if not late:
                    h_lo_of(f, u, it)
                    d_split(D0[f] + u + 2, it)

            def normalise(n, t, coef):
                dve.wait_ge(acc_done, 2 * n + t + 1)
                at = [note(dve.scalar_tensor_tensor(xn[:, t, 512 * h:512 * (h + 1)], ACC[t][h], coef,
                                                    ax[:, t, 512 * h:512 * (h + 1)], ALU.mult, ALU.add)) for h in range(2)]
                for h in range(2):
                    dve.wait_ge(order, at[h])
                    last = dve.bn_stats(stats[:, h, :], xn[:, t, 512 * h:512 * (h + 1)])
                    if h == 0:
                        note(last)
                link(last)
                dve.bn_aggr(mv[:, t, :], stats[:, :, :].rearrange("p a b -> p (a b)")).then_inc(stat_done, 1)
                dve.wait_ge(rstd_done, 2 * n + t + 1)
                dve.tensor_scalar(xn[:, t, :], xn[:, t, :], mv[:, t, 0:1], rstd[:, t, 1:2], ALU.subtract, ALU.mult).then_inc(xn_done, 1)

            def channel_major(e, t):
                for q in range(2):
                    dve.wait_ge(tr_done, 4 * e + 2 * t + q + 1)
                    bank = ps[:, WORK + 2 + q, :].rearrange("p (k s) -> p k s", k=4)
                    if e == 0:
                        last = dve.tensor_copy(xf[:, 4 * q:4 * q + 4, :], bank)
                    else:
                        n = e
                        for k in range(4):
                            last = dve.tensor_scalar(xf[:, 4 * q + k, :], bank[:, k, :], lnT[:, 0, n, 4 * q + k:4 * q + k + 1],
                                                     lnT[:, 1, n, 4 * q + k:4 * q + k + 1], ALU.mult, ALU.add)
                    last.then_inc(xf_done, 1)
                for q in range(2):
                    dve.wait_ge(x_hi_done, 4 * e + 2 * t + q + 1)
                    dst = xT_lo[:, 4 * q:4 * q + 4, t * P:(t + 1) * P]
                    dve.tensor_tensor(dst, xf[:, 4 * q:4 * q + 4, :],
                                      xT_hi[:, 4 * q:4 * q + 4, t * P:(t + 1) * P].bitcast(f32), ALU.subtract).then_inc(x_lo_done, 1)

            def residual(n, t):
                if t == 0:
                    dve.wait_ge(gb_in, 32 * (n + 1))
                    dve.wait_ge(xn_done, 2 * n + 1)
                if t == 1:
                    dve.wait_ge(xn_done, 2 * n + 2)
                link(dve.scalar_tensor_tensor(ax[:, t, :], xn[:, t, :], ALPHA, gb[:, 0, :], ALU.mult, ALU.mult))
                dve.scalar_tensor_tensor(ax[:, t, :], gb[:, 1, :], ALPHA, ax[:, t, :], ALU.mult, ALU.add).then_inc(ax_done, 1)

            dve.wait_ge(lnT_ps, 1)
            dve.tensor_copy(lnT[:, :, :, :].rearrange("p a n k -> p (a n k)"), ps[:, 7, 0:96]).then_inc(lnT_done, 1)
            rotary_tables(dve, link)
            dve.wait_ge(x_in, 16)
            for t in range(TT):
                channel_major(0, t)
                g_split(t)
            for t in range(TT):
                dve.tensor_scalar(ax[:, t, :], xn[:, t, :], ALPHA, None, ALU.mult).then_inc(ax_done, 1)
            for f in range(FFNS):
                for u in range(2):
                    d_split(D0[f] + u)
                if f == 0:
                    for u in range(4):
                        unit(f, u)
                first = 4 if f == 0 else 0
                with dve.Fori(0, (UNITS - 2 - first) // 4) as it:
                    for u in range(first, first + 4):
                        unit(f, u, it)
                for u in range(UNITS - 2, UNITS):
                    unit(f, u)
                n = FFN_NORM[f]
                if f == 0:
                    for t in range(TT):
                        normalise(0, t, 0.5)
                        residual(0, t)
                    dve.wait_ge(aux_in, 32)
                    for k in range(POOL_UNITS):
                        E = D_POOL + k
                        if k == 0:
                            dve.wait_ge(d_in[(E // 2) % 2], 32 * (E // 4 + 1))
                        dve.tensor_tensor(raw_d[:, (E // 2) % 2, E % 2, :], raw_d[:, (E // 2) % 2, E % 2, :], aux[:, 0:D], ALU.mult).then_inc(d_scaled, 1)
                    for c in range(KT // 2):
                        dve.wait_ge(u_hi_done, c + 1)
                        dve.tensor_tensor(xT_lo[:, 2 * c:2 * c + 2, :], ps[:, WORK + c, :].rearrange("p (a s) -> p a s", a=2),
                                          xT_hi[:, 2 * c:2 * c + 2, :].bitcast(f32), ALU.subtract).then_inc(u_lo_done, 1)
                    for k in range(POOL_UNITS):
                        d_split(D_POOL + k)
                    dve.wait_ge(axb_done, 2)
                    for t in range(TT):
                        normalise(1, t, 1.0)
                        channel_major(1, t)
                    for t in range(TT):
                        residual(1, t)
                elif f < 3:
                    for t in range(TT):
                        normalise(n, t, 0.5)
                        channel_major(f + 1, t)
                    for t in range(TT):
                        residual(n, t)
                    if f == 2:
                        attention_dve(dve, link, note, g_split, d_split)
                        dve.wait_ge(axb_done, 4)
                        for t in range(TT):
                            normalise(4, t, 1.0)
                            channel_major(4, t)
                        for t in range(TT):
                            residual(4, t)
                else:
                    for t in range(TT):
                        normalise(5, t, 0.5)
                        if t == 0:
                            dve.wait_ge(gb_in, 32 * 6)
                        dve.wait_ge(xn_done, 10 + t + 1)
                        for h in range(2):
                            y = xn[:, t, 512 * h:512 * (h + 1)]
                            link(dve.tensor_tensor(y, y, gb[:, 0, 512 * h:512 * (h + 1)], ALU.mult))
                            dve.tensor_tensor(y, y, gb[:, 1, 512 * h:512 * (h + 1)], ALU.add).then_inc(y_done, 1)

        def pool_pe(pe, three):
            pe.wait_ge(band_in, 16)
            pe.wait_ge(hf_done, UNITS)
            for c in range(KT // 2):
                for k in (2 * c, 2 * c + 1):
                    b = band[:, k // 2, :]
                    o = ps[:, WORK + c, (k % 2) * S:(k % 2 + 1) * S]
                    if k == 0:
                        pe.wait_ge(ax_done, 3)
                    ins = pe.matmul(o[:, 0:P], ax[:, 0, k * P:(k + 1) * P], b[:, 0:P], start=True, stop=True)
                    if k == 0:
                        ins.then_inc(d_used, 1)
                    if k == 0:
                        pe.wait_ge(ax_done, 4)
                    pe.matmul(o[:, P:2 * P], ax[:, 1, k * P:(k + 1) * P], b[:, P:2 * P], start=True, stop=False)
                    last = pe.matmul(o[:, P:P + 16], ax[:, 0, k * P:(k + 1) * P], b[:, 2 * P:2 * P + 16], start=False, stop=True)
                last.then_inc(u_done, 1)
            for t in range(TT):
                for g in range(len(WINDOWS)):
                    for j in range(2):
                        k, E = 2 * g + j, D_POOL + j
                        if t == 0:
                            pe.wait_ge(u_lo_done, g + 1)
                            if g == 0:
                                pe.wait_ge(d_lo_done, E + 1)
                        tok = slice(t * P, (t + 1) * P)
                        w_hi, w_lo = (b[:, E % D_SLOTS, g * GC:(g + 1) * GC] for b in (d_hi, d_lo))
                        last = three(ACC[t][g // 2][:, (g % 2) * GC:(g % 2 + 1) * GC], xT_hi[:, k, tok], xT_lo[:, k, tok],
                                     w_hi, w_lo, j == 0, j == 1)
                last.then_inc(acc_done, 1)

        def attention_pe(pe, three, down, transposes):
            ident = cst[:, 0, :]
            e = QKV_EVENT

            def qkv(c, half, t, used=False):
                G = G_QKV + 2 * c + half
                bank = ps[:, (2 * c + t) % 4, :]
                if t == 0:
                    pe.wait_ge(g_lo_done, 2 * G + 2)
                    if c == 2 and half == 0:
                        pe.wait_ge(qkv_sb, 1)
                if c == 0:
                    pe.wait_ge(x_lo_done, 4 * e + 2 * t + half + 1)
                tok = slice(t * P, (t + 1) * P)
                for j in range(4):
                    w_hi, w_lo = (b[:, G % G_SLOTS, 512 * j:512 * (j + 1)] for b in (g_hi, g_lo))
                    k = 4 * half + j
                    x_hi, x_lo = xT_hi[:, k, tok], xT_lo[:, k, tok]
                    ins = pe.matmul(bank, x_hi, w_hi, start=k == 0, stop=False)
                    if j == 0 and used:
                        ins.then_inc(g_used, 1)
                    pe.matmul(bank, x_hi, w_lo, start=False, stop=False)
                    last = pe.matmul(bank, x_lo, w_hi, start=False, stop=k == KT - 1)
                return last

            def to_channels(c):
                if c == 0:
                    pe.wait_ge(dup_done, 1)
                    pe.wait_ge(xf_done, 4 * e + 4)
                else:
                    pe.wait_ge(qkv_sb, c + 1)
                    pe.wait_ge(qkT_done, 2 * c)
                if c == 2:
                    pe.wait_ge(oT_lo_done, 1)
                for t in range(TT):
                    for j in range(4):
                        src = kd[:, t, j, :, :].rearrange("p e d -> p (e d)") if c == 0 else xn[:, t, 512 * (c - 1) + P * j:512 * (c - 1) + P * (j + 1)]
                        last = pe.transpose(ps[:, WORK + 2 + t, P * j:P * (j + 1)], src, ident)
                    last.then_inc(qkT_ps, 1)

            def scores(i):
                g, n = TASKS[i]
                if i == 0:
                    pe.wait_ge(qkT_done, 4)
                    pe.wait_ge(hf_done, 3 * UNITS)
                if i == 4:
                    pe.wait_ge(qkT_done, 6)
                after(pe, s_sb, i)
                for h in range(4):
                    head = 4 * g + h
                    keys = slice(0, (n + 1) * P)
                    o = ps[:, WORK, P * h:P * (h + 1)] if n == 0 else two_banks[:, h, :]
                    last = pe.matmul(o, qT[:, head // 2, n * P:(n + 1) * P], kT[:, g, head % 2, keys], start=True, stop=True)
                    if i == 1 and h == 0:
                        last.then_inc(g_used, 1)
                last.then_inc(s_done, 1)

            def probs_T(i):
                pe.wait_ge(p_done, i + 1)
                for h in range(4):
                    last = pe.transpose(ps[:, WORK + 2, P * h:P * (h + 1)], sc[i % 2][:, h, :], ident)
                last.then_inc(pT_ps, 1)

            def values(i):
                g, n = TASKS[i]
                pe.wait_ge(pT_a if n == 0 else pT_v, g + 1)
                after(pe, oT_lo_done, i)
                o = ps[:, WORK + 3, :]
                own = pT[i % 2][:, 1].rearrange("p h q -> p (h q)")
                prev = pT[i % 2][:, 0].rearrange("p h q -> p (h q)")
                v = [vd[:, t, g, :, :].rearrange("p e d -> p (e d)") for t in range(TT)]
                if n == 1:
                    pe.matmul(o, v[0], prev, start=True, stop=False)
                pe.matmul(o, v[n], own, start=n == 0, stop=True).then_inc(oT_ps, 1)

            def wo(k, ts=(0, 1), norm=False):
                if ts[0] == 0:
                    pe.wait_ge(oT_lo_done, 2 * (k // 2) + (2 if ts[-1] == 1 else 1))
                    if k == 0:
                        pe.wait_ge(qkv_sb, 3)
                else:
                    pe.wait_ge(oT_lo_done, 2 * (k // 2) + 2)
                last = down(D_WO + k, xT_hi[:, k, :], xT_lo[:, k, :], ts, k == 0, k == WO_UNITS - 1)
                if norm:
                    last.then_inc(acc_done, 1)
                elif ts[-1] == 1:
                    last.then_inc(d_used, 1)

            transposes(e, 0, used=1)
            qkv(0, 0, 0)
            transposes(e, 1)
            qkv(0, 1, 0).then_inc(qkv_done, 1)
            qkv(0, 0, 1).then_inc(g_used, 1)
            qkv(0, 1, 1).then_inc(qkv_done, 1)
            for c in (1, 2):
                qkv(c, 0, 0, used=True)
                qkv(c, 0, 1).then_inc(g_used, 1)
                if c == 1:
                    to_channels(0)
                    qkv(c, 1, 0).then_inc(qkv_done, 1)
                    qkv(c, 1, 1).then_inc(qkv_done, 1)
                else:
                    to_channels(1)
                    scores(0)
                    qkv(c, 1, 0).then_inc(qkv_done, 1)
                    qkv(c, 1, 1).then_inc(qkv_done, 1)
            for i in range(len(TASKS)):
                if i + 1 < len(TASKS):
                    scores(i + 1)
                if i == 1:
                    to_channels(2)
                if i == 1:
                    pe.wait_ge(qkT_done, 6)
                probs_T(i)
                if i >= 2:
                    wo(i - 2)
                values(i)
            wo(6, (0,))
            wo(7, (0,), norm=True)
            wo(6, (1,))
            wo(7, (1,), norm=True)


        @block.tensor
        def _(pe):
            ident = cst[:, 0, :]

            def three(out_, l_hi, l_lo, r_hi, r_lo, start, stop):
                pe.matmul(out_, l_hi, r_hi, start=start, stop=False)
                pe.matmul(out_, l_hi, r_lo, start=False, stop=False)
                return pe.matmul(out_, l_lo, r_hi, start=False, stop=stop)

            def gate_up(f, u, ts, e=None, it=0):
                G = G0[f] + u
                lo_t, hi_t = ts[0] * P, (ts[-1] + 1) * P
                if ts[0] == 0:
                    pe.wait_ge(g_lo_done, 2 * G + 2 + 8 * it)
                    after(pe, hf_done, UNITS * f + u - 1 + 4 * it)
                for m in range(2):
                    for k in range(KT):
                        if e is not None and m == 0 and k % 4 == 0:
                            pe.wait_ge(x_lo_done, 4 * e + 2 * ts[0] + k // 4 + 1)
                        w_hi, w_lo = g_half(g_hi, G, m)[:, k, :], g_half(g_lo, G, m)[:, k, :]
                        last = three(ps[:, WORK + u % 2, m * S + lo_t:m * S + hi_t], w_hi, w_lo,
                                     xT_hi[:, k, lo_t:hi_t], xT_lo[:, k, lo_t:hi_t], k == 0, k == KT - 1)
                if ts[-1] == TT - 1:
                    last.then_inc(g_used, 1)

            def down(E, l_hi, l_lo, ts, first, final, it=0):
                if ts[0] == 0:
                    pe.wait_ge(d_lo_done, E + 1 + 4 * it)
                for t in ts:
                    for h in range(2):
                        w_hi, w_lo = (b[:, E % D_SLOTS, 512 * h:512 * (h + 1)] for b in (d_hi, d_lo))
                        tok = slice(t * P, (t + 1) * P)
                        last = three(ACC[t][h], l_hi[:, tok], l_lo[:, tok], w_hi, w_lo, first, final)
                return last

            def ffn_down(f, u, ts=(0, 1), it=0, norm=None):
                if ts[0] == 0:
                    pe.wait_ge(h_lo_done, UNITS * f + u + 1 + 4 * it)
                E = D0[f] + u
                final = u == UNITS - 1 and norm is not None
                last = down(E, hT_hi[:, E % D_SLOTS, :], hT_lo[:, E % D_SLOTS, :], ts, u == 0, final, it)
                if final:
                    last.then_inc(acc_done, 1)
                elif ts[-1] == TT - 1:
                    last.then_inc(d_used, 1)

            def transposes(e, t, used=0):
                for q in range(2):
                    if q == 0 and e > 0:
                        pe.wait_ge(xn_done, 2 * e + t + 1)
                    after(pe, xf_done, 4 * e + 2 * t + q - 1)
                    for k in range(4 * q, 4 * q + 4):
                        last = pe.transpose(ps[:, WORK + 2 + q, (k % 4) * P:(k % 4 + 1) * P], xn[:, t, k * P:(k + 1) * P], ident)
                        if k == 0 and used:
                            last.then_inc(d_used, used)
                    last.then_inc(tr_done, 1)

            pe.wait_ge(cst_in, 16)
            pe.wait_ge(small_in, 64)
            for a in range(2):
                last = pe.transpose(ps[:, 7, 48 * a:48 * (a + 1)], lnrow[:, a, :], ident[0:48, 0:48])
            last.then_inc(lnT_ps, 1)
            pe.wait_ge(x_in, 16)
            pe.wait_ge(lnT_done, 1)
            for f in range(FFNS):
                e = FFN_EVENT[f]
                transposes(e, 0, used=(0, 2, 1, 1)[f])
                gate_up(f, 0, (0,), e)
                transposes(e, 1)
                gate_up(f, 1, (0,))
                gate_up(f, 0, (1,), e)
                gate_up(f, 1, (1,))
                ffn_down(f, 0)
                with pe.Fori(0, (UNITS - 6) // 4) as it:
                    for u in range(2, 6):
                        gate_up(f, u, (0, 1), it=it)
                        ffn_down(f, u - 1, it=it)
                last_u = UNITS - 4
                gate_up(f, last_u, (0, 1))
                ffn_down(f, last_u - 1)
                gate_up(f, last_u + 1, (0, 1))
                ffn_down(f, last_u, (0,))
                gate_up(f, last_u + 2, (0, 1))
                ffn_down(f, last_u + 1, (0,))
                gate_up(f, last_u + 3, (0, 1))
                ffn_down(f, last_u + 2, (0,))
                ffn_down(f, last_u, (1,))
                ffn_down(f, last_u + 3, (0,), norm=FFN_NORM[f])
                ffn_down(f, last_u + 1, (1,))
                ffn_down(f, last_u + 2, (1,))
                ffn_down(f, last_u + 3, (1,), norm=FFN_NORM[f])
                if f == 0:
                    pool_pe(pe, three)
                if f == 2:
                    attention_pe(pe, three, down, transposes)

_INS = ["x", "positions", "ln_g", "ln_b", "ffn_w_gate", "ffn_w_up", "ffn_w_down", "pool_w", "pool_b", "pool_scale",
        "attn_w_qkv", "attn_b_qkv", "attn_sinks", "attn_w_o", "attn_b_o"]


def pool_bands():
    full = np.zeros((4, S, S), np.float64)
    for g, win in enumerate(WINDOWS):
        for s in range(S):
            lo = max(s + 1 - win, 0)
            full[g, lo:s + 1, s] = 1.0 / (s + 1 - lo)
            full[g, s, s] -= 1.0
    full /= ALPHA
    return np.concatenate([full[:, :P, :P], full[:, P:, P:], full[:, :P, P:P + 16]], axis=2).astype(np.float32)


def attention_masks():
    q, j = np.arange(P)[:, None], np.arange(P)[None, :]
    eye = (q == j)
    return np.stack([eye, (j > q) * NEG, j > q, j >= q]).astype(np.float32)


def kernel(**inputs):
    import concourse.bacc as bacc
    from concourse.bass_utils import run_bass_kernel_spmd

    nc = bacc.Bacc("TRN2", target_bir_lowering=False, num_devices=1)
    arrays, args = {}, []
    named = [(n, inputs[n]) for n in _INS] + [("bands", pool_bands()), ("masks", attention_masks())]
    for name, a in named:
        a = np.ascontiguousarray(a)
        arrays[f"in_{name}"] = a
        args.append(nc.dram_tensor(f"in_{name}", a.shape, mybir.dt.from_np(a.dtype), kind="ExternalInput").ap())
    args.append(nc.dram_tensor("out_y", (1, S, D), mybir.dt.float32, kind="ExternalOutput").ap())
    trunk_kernel(nc, *args)
    r = run_bass_kernel_spmd(nc, [arrays], core_ids=[0])
    return r.results[0]["out_y"]
```

```python
import math
from contextlib import ExitStack

import numpy as np

import concourse.bass as bass
from concourse import mybir

P = 128
D = 1024
S = 256
F = 2816
KT = D // P
TT = S // P
UNITS = F // P
FFNS = 4
HD = 64
NQ = 16
NKV = 4
ROT = 16
HALF = ROT // 2
THETA = 500000.0
WINDOWS = (2, 4, 8, 16)
GC = D // len(WINDOWS)
ALPHA = 4.0 ** 0.25
EPS = 1e-5
SCALE = HD ** -0.5
NEG = -1e30
LAST = 3

QKV_UNITS = 6
POOL_UNITS = 2
WO_UNITS = 8
RAW_UNITS = 2
G0 = [0, UNITS, 2 * UNITS, 3 * UNITS + QKV_UNITS]
D0 = [0, UNITS + POOL_UNITS, 2 * UNITS + POOL_UNITS, 3 * UNITS + POOL_UNITS + WO_UNITS]
G_QKV = 3 * UNITS
D_POOL = UNITS
D_WO = 3 * UNITS + POOL_UNITS
X0 = [-2, UNITS - 4, 2 * UNITS - 6, 3 * UNITS - 8 + QKV_UNITS]
X_QKV = 3 * (UNITS - RAW_UNITS)
G_SLOTS = 2
D_SLOTS = 4

T_EVENT = {1: 1, 2: 2, 3: 3, 4: 4}
FFN_NORM = [0, 2, 3, 5]
FFN_EVENT = [0, 1, 2, 4]
QKV_EVENT = 3


def trunk_kernel(nc, x, positions, ln_g, ln_b, w_gate, w_up, w_down, pool_w, pool_b, pool_scale,
                 w_qkv, b_qkv, sinks, w_o, b_o, bands, masks, out):
    f32 = mybir.dt.float32
    f32r = mybir.dt.float32r
    i32 = mybir.dt.int32
    ALU = mybir.AluOpType
    ACT = mybir.ActivationFunctionType
    AX = mybir.AxisListType

    with ExitStack() as ctx:
        def sb(name, shape, dt=f32):
            return ctx.enter_context(nc.sbuf_tensor(name, shape, dt))

        def sem(name):
            return ctx.enter_context(nc.semaphore(name))

        raw_g = sb("raw_g", [P, 2, 2, 2048])
        raw_d = sb("raw_d", [P, 2, 2, 1024])
        g_hi = sb("g_hi", [P, G_SLOTS, 2048], f32r)
        g_lo = sb("g_lo", [P, G_SLOTS, 2048], f32r)
        d_hi = sb("d_hi", [P, D_SLOTS, 1024], f32r)
        d_lo = sb("d_lo", [P, D_SLOTS, 1024], f32r)
        xT_hi = sb("xT_hi", [P, KT, S], f32r)
        xT_lo = sb("xT_lo", [P, KT, S], f32r)
        hT_hi = sb("hT_hi", [P, D_SLOTS, S], f32r)
        hT_lo = sb("hT_lo", [P, D_SLOTS, S], f32r)
        xn = sb("xn", [P, TT, D])
        ax = sb("ax", [P, TT, D])
        xf = sb("xf", [P, TT, KT, P])
        silu = sb("silu", [P, 2, S])
        hf = sb("hf", [P, 2, S])
        gb = sb("gb", [P, 2, D])
        aux = sb("aux", [P, 2560])
        cst = sb("cst", [P, 4, P])
        lnT = sb("lnT", [P, 2, 6, KT])
        lnrow = ax[0:6 * KT, 1, 0:2 * P].rearrange("p (a c) -> p a c", a=2)
        stats = sb("stats", [P, 2, 6])
        mv = sb("mv", [P, 2, 2])
        rstd = sb("rstd", [P, 2, 2])
        mhalf = sb("mhalf", [P, 1])
        pos_i = sb("pos_i", [P, TT], i32)
        ang = sb("ang", [P, 8, TT, HALF])
        invf = sb("invf", [P, HALF])
        rot = sb("rot", [P, TT, 3, HALF])
        sinkb = sb("sinkb", [P, NQ])
        sm = sb("sm", [P, 2, 6, 4])
        vd = sb("vd", [P, TT, NKV, 2, HD])
        qT = sb("qT", [P, KT, S])
        kT = sb("kT", [P, NKV, 2, S])
        band = qT[:, :, :].rearrange("p k s -> p (k s)")[:, 0:4 * 384].rearrange("p (g c) -> p g c", g=4)
        kd = xf[:, 0].rearrange("p k s -> p (k s)").rearrange("p (t g e d) -> p t g e d", t=TT, g=NKV, e=2)
        sc = [silu[:, :, :].rearrange("p a s -> p (a s)").rearrange("p (h j) -> p h j", h=4),
              hf[:, :, :].rearrange("p a s -> p (a s)").rearrange("p (h j) -> p h j", h=4)]
        pT = [gb[:, i, :].rearrange("p (b h q) -> p b h q", b=2, h=4) for i in range(2)]

        ps = ctx.enter_context(nc.psum_tensor("ps", [P, 8, 512], f32))
        ACC = [[ps[:, 2 * t + h, :] for h in range(2)] for t in range(TT)]
        WORK = 4

        g_in = [sem("g_in0"), sem("g_in1")]
        d_in = [sem("d_in0"), sem("d_in1")]
        g_hi_done = sem("g_hi_done")
        g_lo_done = sem("g_lo_done")
        d_hi_done = sem("d_hi_done")
        d_lo_done = sem("d_lo_done")
        d_scaled = sem("d_scaled")
        g_used = sem("g_used")
        d_used = sem("d_used")
        silu_done = sem("silu_done")
        hf_done = sem("hf_done")
        h_hi_done = sem("h_hi_done")
        h_lo_done = sem("h_lo_done")
        acc_done = sem("acc_done")
        stat_done = sem("stat_done")
        var_done = sem("var_done")
        rstd_done = sem("rstd_done")
        xn_done = sem("xn_done")
        tr_done = sem("tr_done")
        xf_lo_done = sem("xf_lo_done")
        xf_up_done = sem("xf_up_done")
        x_hi_done = sem("x_hi_done")
        x_lo_done = sem("x_lo_done")
        ax_done = sem("ax_done")
        u_done = sem("u_done")
        u_hi_done = sem("u_hi_done")
        u_lo_done = sem("u_lo_done")
        axb_done = sem("axb_done")
        res_step = sem("res_step")
        bs_done = sem("bs_done")
        x_in = [sem("x_in0"), sem("x_in1")]
        small_in = sem("small_in")
        band_in = sem("band_in")
        gb_in = sem("gb_in")
        aux_in = sem("aux_in")
        cst_in = sem("cst_in")
        consts = sem("consts")
        lnT_ps = sem("lnT_ps")
        lnT_done = sem("lnT_done")
        kz_done = sem("kz_done")
        ang_done = sem("ang_done")
        sin_done = sem("sin_done")
        order = sem("dve_order")
        qkv_done = sem("qkv_done")
        qkv_sb = sem("qkv_sb")
        dup_done = sem("dup_done")
        qkT_ps = sem("qkT_ps")
        qkT_done = sem("qkT_done")
        s_done = sem("s_done")
        diag_done = sem("diag_done")
        s_sb = sem("s_sb")
        m_done = sem("m_done")
        e_done = sem("e_done")
        p_done = sem("p_done")
        pT_ps = sem("pT_ps")
        pT_a = sem("pT_a")
        pT_v = sem("pT_v")
        oT_ps = sem("oT_ps")
        oT_hi_done = sem("oT_hi_done")
        oT_lo_done = sem("oT_lo_done")
        y_done = sem("y_done")
        out_done = sem("out_done")

        TASKS = [(g, n) for g in range(NKV) for n in range(TT)]

        def after(eng, s, value):
            if not isinstance(value, int) or value > 0:
                eng.wait_ge(s, value)

        def raw_unit(G, half):
            c = raw_g[:, (G // 2) % 2, half, :].rearrange("p (k f) -> p k f", k=KT)
            return c[:, :, (G % 2) * P:(G % 2 + 1) * P]

        def raw_qkv(G, half):
            return raw_g[:, (G // 2) % 2, G % 2, half * 1024:(half + 1) * 1024].rearrange("p (k f) -> p k f", k=KT)

        def g_half(buf, X, half):
            return buf[:, X % G_SLOTS, half * 1024:(half + 1) * 1024].rearrange("p (k f) -> p k f", k=KT)

        def split_unit(f, u):
            return (X_QKV + u, G_QKV + u, raw_qkv) if f is None else (X0[f] + u, G0[f] + u, raw_unit)

        two_banks = ps[:, WORK:WORK + 2, :].rearrange("p b (h j) -> p (b h) j", h=2)
        axb = xf[:, :, :, :].rearrange("p t k s -> p t (k s)")
        rtmp = xf[:, 1, 0:2, :].rearrange("p a (h j) -> p a h j", h=8)
        prevT = xf[:, 1, 2:3, :]

        block = ctx.enter_context(nc.Block())

        @block.sync
        def _(sp):
            gate_v = w_gate.rearrange("l i (k p) f -> (l i) p k f", p=P)
            up_v = w_up.rearrange("l i (k p) f -> (l i) p k f", p=P)
            down_v = w_down.rearrange("l i (u p) d -> (l i) p u d", p=P)
            qkv_v = w_qkv[0].rearrange("(k p) c -> p k c", p=P)
            wo_v = w_o[0].rearrange("(u p) d -> p u d", p=P)
            pool_v = pool_w[0].rearrange("g (k p) d -> p k g d", p=P)

            def load_ffn(f, c, it):
                C, E = G0[f] // 2 + c, D0[f] // 2 + c
                if c == 2:
                    sp.wait_ge(g_used, G0[f] + RAW_UNITS)
                elif c > 2:
                    sp.wait_ge(g_lo_done, 2 * (X0[f] + 2 * c - 2) + 8 * it)
                elif f > 0:
                    sp.wait_ge(g_lo_done, 2 * (X0[f] + 2 * c))
                dst = raw_g[:, C % 2, :, :].rearrange("p m (k f) -> p m k f", k=KT)
                for m, w in enumerate((gate_v, up_v)):
                    sp.dma_start(dst[:, m], w[f, :, :, bass.ds(2 * P * c + 4 * P * it, 2 * P)]).then_inc(g_in[C % 2], 16)
                after(sp, d_lo_done, 2 * (E - 1) + 4 * it)
                for m in range(2):
                    sp.dma_start(raw_d[:, E % 2, m, :], down_v[f, :, bass.ds(2 * c + m + 4 * it, 1), :].rearrange("p a d -> p (a d)")).then_inc(d_in[E % 2], 16)

            def load_d(E, srcs):
                after(sp, d_lo_done, 2 * (E - 1))
                for m, src in enumerate(srcs):
                    dst = raw_d[:, E % 2, m, :]
                    sp.dma_start(dst.rearrange("p (g d) -> p g d", g=4) if len(src.shape) == 3 else dst, src).then_inc(d_in[E % 2], 16)

            sp.dma_start(cst[:, :, :], masks.rearrange("m p q -> p m q")).then_inc(cst_in, 16)
            for t in range(TT):
                sp.dma_start(xn[:, t, :], x[0, t * P:(t + 1) * P, :]).then_inc(x_in[t], 16)
            for f in range(FFNS):
                for c in range(3):
                    load_ffn(f, c, 0)
                with sp.Fori(0, (UNITS // 2 - 3) // 2) as it:
                    for c in range(3, 5):
                        load_ffn(f, c, it)
                if f == 0:
                    load_d(D_POOL // 2, [pool_v[:, k] for k in range(2)])
                if f == 2:
                    for i, j in enumerate((2, 0, 1)):
                        C = G_QKV // 2 + i
                        sp.wait_ge(g_lo_done, 2 * (X_QKV - 2 + 2 * i))
                        for m in range(2):
                            sp.dma_start(raw_g[:, C % 2, m, :].rearrange("p (k c) -> p k c", k=4),
                                         qkv_v[:, 4 * m:4 * m + 4, 512 * j:512 * (j + 1)]).then_inc(g_in[C % 2], 16)
                        if i < 2:
                            load_d(D_WO // 2 + i, [wo_v[:, 2 * i + m] for m in range(2)])
                    for i in range(2, 4):
                        load_d(D_WO // 2 + i, [wo_v[:, 2 * i + m] for m in range(2)])
            for t in range(TT):
                for h in range(2):
                    sp.wait_ge(y_done, 2 * t + h + 1)
                    sp.dma_start(out[0, t * P:(t + 1) * P, 512 * h:512 * (h + 1)], xn[:, t, 512 * h:512 * (h + 1)]).then_inc(out_done, 16)
            sp.wait_ge(out_done, 64)

        @block.gpsimd
        def _(gp):
            gp.dma_start(band[:, :, :], bands.rearrange("g p c -> p g c")).then_inc(band_in, 16)
            for j in range(HALF):
                gp.memset(invf[:, j:j + 1], float(np.float32(THETA) ** np.float32(-2.0 * j / ROT)))
            gp.memset(mhalf[:, :], -0.5).then_inc(consts, 1)
            gp.memset(kT[:, :, :, :], 0.0).then_inc(kz_done, 1)
            gp.dma_start(aux[:, 0:D], pool_scale[0:1, :].to_broadcast([P, D])).then_inc(aux_in, 16)
            gp.dma_start(aux[:, D:2 * D], pool_b[0:1, :].to_broadcast([P, D])).then_inc(aux_in, 16)
            gp.wait_ge(aux_in, 32)
            gp.tensor_tensor(aux[:, D:2 * D], aux[:, D:2 * D], aux[:, 0:D], ALU.mult).then_inc(bs_done, 1)

            for n in range(6):
                if n > 0:
                    gp.wait_ge(ax_done, 2 * n + 2)
                if n == 4:
                    gp.wait_ge(oT_ps, len(TASKS))
                gp.dma_start(gb[:, 0, :], ln_g[n // 3, n % 3:n % 3 + 1, :].to_broadcast([P, D])).then_inc(gb_in, 16)
                gp.dma_start(gb[:, 1, :], ln_b[n // 3, n % 3:n % 3 + 1, :].to_broadcast([P, D])).then_inc(gb_in, 16)
                if n == 0:
                    for k in range(POOL_UNITS):
                        raw = raw_d[:, (D_POOL // 2) % 2, k, :]
                        if k == 0:
                            gp.wait_ge(d_in[(D_POOL // 2) % 2], 32 * (D_POOL // 4 + 1))
                        gp.tensor_tensor(raw, raw, aux[:, 0:D], ALU.mult).then_inc(d_scaled, 1)
                    gp.wait_ge(bs_done, 1)
                if n == 3:
                    gp.wait_ge(gb_in, 32 * (n + 1))
                    gp.tensor_scalar(gb[:, :, :], gb[:, :, :], ALPHA, None, ALU.mult).then_inc(res_step, 1)
                    gp.wait_ge(res_step, 1)
                    gp.wait_ge(aux_in, 64)
                    gp.tensor_tensor(gb[:, 1, :], gb[:, 1, :], aux[:, 1536:2560], ALU.add).then_inc(res_step, 1)
                    gp.wait_ge(res_step, 2)
                for t in range(TT):
                    gp.wait_ge(stat_done, 2 * n + t + 1)
                    gp.tensor_scalar(rstd[:, t, 0:1], mv[:, t, 1:2], EPS, None, ALU.add).then_inc(var_done, 1)
                    gp.wait_ge(var_done, 2 * n + t + 1)
                    gp.tensor_tensor(rstd[:, t, 1:2], rstd[:, t, 0:1], mhalf[:, :], ALU.pow).then_inc(rstd_done, 1)
                    if n == 3:
                        gp.wait_ge(xn_done, 4 * n + 2 * t + 2)
                        gp.tensor_tensor(ax[:, t, :], xn[:, t, :], gb[:, 0, :], ALU.mult).then_inc(res_step, 1)
                        gp.wait_ge(res_step, 3 + t)
                        gp.tensor_tensor(ax[:, t, :], ax[:, t, :], gb[:, 1, :], ALU.add).then_inc(ax_done, 1)
                if n == 0:
                    for t in range(TT):
                        gp.wait_ge(ax_done, 2 * (n + 1) + t + 1)
                        gp.tensor_tensor(axb[:, t, :], ax[:, t, :], aux[:, D:2 * D], ALU.add).then_inc(axb_done, 1)
                if n == 1:
                    gp.wait_ge(axb_done, 2)
                    gp.dma_start(aux[:, 0:1536], b_qkv[0:1, :].to_broadcast([P, 1536])).then_inc(aux_in, 16)
                    gp.dma_start(aux[:, 1536:2560], b_o[0:1, :].to_broadcast([P, D])).then_inc(aux_in, 16)

        def attention_act(act, g_split, d_split):
            def wo_split(k):
                d_split(D_WO + k)

            def duplicate(t):
                act.wait_ge(qkv_sb, t + 1)
                act.activation(kd[:, t, :, 1, :], kd[:, t, :, 0, :], ACT.Copy)
                act.activation(vd[:, t, :, 1, :], vd[:, t, :, 0, :], ACT.Copy).then_inc(dup_done, 1)

            def transposed(c, t):
                act.wait_ge(qkT_ps, 2 * c + t + 1)
                bank = ps[:, (2 if c == 2 else WORK + 2) + t, :].rearrange("p (a s) -> p a s", a=4)
                if c == 0:
                    if t == 0:
                        act.wait_ge(kz_done, 1)
                    act.activation(kT[0:HD, :, 0, t * P:(t + 1) * P], bank[0:HD], ACT.Copy)
                    act.activation(kT[HD:P, :, 1, t * P:(t + 1) * P], bank[HD:P], ACT.Copy).then_inc(qkT_done, 1)
                else:
                    act.activation(qT[:, 4 * c - 4:4 * c, t * P:(t + 1) * P], bank, ACT.Copy).then_inc(qkT_done, 1)

            def diag(i):
                g, n = TASKS[i]
                if n == 1:
                    act.wait_ge(s_done, i + 1)
                    after(act, pT_ps, i - 1)
                    act.activation(sc[i % 2][:, :, :], two_banks[:, :, P:2 * P], ACT.Copy).then_inc(diag_done, 1)

            def exps(i):
                act.wait_ge(m_done, i + 1)
                for h in range(4):
                    act.activation(sc[i % 2][:, h, :], sc[i % 2][:, h, :], ACT.Exp, bias=sm[:, i % 2, 1, h:h + 1],
                                   scale=SCALE, accum_out=sm[:, i % 2, 3, h:h + 1])
                act.activation(sm[:, i % 2, 4, :], sm[:, i % 2, 2, :], ACT.Exp).then_inc(e_done, 1)

            def pT_copy(i):
                if TASKS[i][1] == 0:
                    act.wait_ge(pT_ps, i + 1)
                    if i == 0:
                        act.wait_ge(ax_done, 10)
                    act.activation(pT[i % 2][:, 1], ps[:, WORK + 2, :].rearrange("p (h q) -> p h q", h=4), ACT.Copy).then_inc(pT_a, 1)

            def o_hi(i):
                g, n = TASKS[i]
                act.wait_ge(oT_ps, i + 1)
                bank = ps[:, WORK + 3, :].rearrange("p (a e q) -> p a e q", a=2, e=2)
                act.activation(xT_hi[0:HD, 2 * g:2 * g + 2, n * P:(n + 1) * P], bank[0:HD, :, 0, :], ACT.Copy)
                act.activation(xT_hi[HD:P, 2 * g:2 * g + 2, n * P:(n + 1) * P], bank[HD:P, :, 1, :], ACT.Copy).then_inc(oT_hi_done, 1)

            duplicate(0)
            g_split(None, 2)
            g_split(None, 3)
            duplicate(1)
            wo_split(0)
            wo_split(1)
            g_split(None, 4)
            transposed(0, 0)
            transposed(0, 1)
            transposed(1, 0)
            g_split(None, 5)
            transposed(1, 1)
            exps(0)
            for i in range(len(TASKS)):
                if i >= 1:
                    o_hi(i - 1)
                if i >= 2:
                    wo_split(i)
                if i == 2:
                    transposed(2, 0)
                    transposed(2, 1)
                if i + 1 < len(TASKS):
                    diag(i + 1)
                pT_copy(i)
                if i + 1 < len(TASKS):
                    exps(i + 1)
            o_hi(len(TASKS) - 1)

        @block.scalar
        def _(act):
            def g_split(f, u, it=0):
                X, G, src = split_unit(f, u)
                act.wait_ge(g_in[(G // 2) % 2], 32 * (G // 4 + 1) + 32 * it)
                after(act, g_used, (G0[f] + u - 3 if f is not None and u < 4 else G - 1) + 4 * it)
                for half in range(2):
                    act.activation(g_half(g_hi, X, half), src(G, half), ACT.Copy).then_inc(g_hi_done, 1)

            def d_split(E, it=0):
                act.wait_ge(d_in[(E // 2) % 2], 32 * (E // 4 + 1) + 32 * it)
                after(act, d_used, E - D_SLOTS + 1 + 4 * it)
                act.activation(d_hi[:, E % D_SLOTS, :], raw_d[:, (E // 2) % 2, E % 2, :], ACT.Copy).then_inc(d_hi_done, 1)

            def silu_of(f, u, it=0):
                act.wait_ge(g_used, G0[f] + u + 1 + 4 * it)
                act.activation(silu[:, u % 2, :], ps[:, WORK + u % 2, 0:S], ACT.Silu).then_inc(silu_done, 1)

            def h_hi_of(f, u, it=0):
                act.wait_ge(hf_done, UNITS * f + u + 1 + 4 * it)
                act.activation(hT_hi[:, (D0[f] + u) % D_SLOTS, :], hf[:, u % 2, :], ACT.Copy).then_inc(h_hi_done, 1)

            def unit(f, u, it=0):
                silu_of(f, u, it)
                if 1 <= u < UNITS - 2:
                    g_split(f, u + 2, it)
                h_hi_of(f, u, it)
                if u + 1 < UNITS:
                    d_split(D0[f] + u + 1, it)

            def channel_major(e):
                for t in range(TT):
                    act.wait_ge(tr_done, 4 * e + 2 * t + 2)
                    bank = ps[:, WORK + 3, :].rearrange("p (k s) -> p k s", k=4)
                    if e == 0:
                        last = act.activation(xf[:, t, 4:8, :], bank, ACT.Copy)
                    else:
                        for k in range(4, 8):
                            last = act.activation(xf[:, t, k, :], bank[:, k - 4, :], ACT.Identity, bias=lnT[:, 1, e, k:k + 1],
                                                  scale=lnT[:, 0, e, k:k + 1])
                    last.then_inc(xf_up_done, 1)
                    if e == QKV_EVENT:
                        x_hi(e, t)
                if e != QKV_EVENT:
                    for t in range(TT):
                        x_hi(e, t)

            def x_hi(e, t):
                for q, ready in enumerate((xf_lo_done, xf_up_done)):
                    act.wait_ge(ready, 2 * e + t + 1)
                    act.activation(xT_hi[:, 4 * q:4 * q + 4, t * P:(t + 1) * P], xf[:, t, 4 * q:4 * q + 4, :], ACT.Copy).then_inc(x_hi_done, 1)

            act.dma_start(lnrow[:, 0, :], ln_g.rearrange("l n (k p) -> (l n k) p", p=P)).then_inc(small_in, 16)
            act.dma_start(lnrow[:, 1, :], ln_b.rearrange("l n (k p) -> (l n k) p", p=P)).then_inc(small_in, 16)
            act.dma_start(pos_i[:, :], positions[0].rearrange("(t p) -> p t", p=P), allow_slow_non_contiguous=True).then_inc(small_in, 16)
            act.dma_start(sinkb[:, :], sinks[0:1, :].to_broadcast([P, NQ])).then_inc(small_in, 16)
            act.wait_ge(lnT_done, 1)
            channel_major(0)
            act.wait_ge(ang_done, 1)
            act.activation(rot[:, :, 1, :], ang[:, 0], ACT.Sin)
            act.activation(rot[:, :, 0, :], ang[:, 1], ACT.Sin).then_inc(sin_done, 1)
            g_split(0, RAW_UNITS)
            for f in range(FFNS):
                d_split(D0[f])
                for u in range(4):
                    unit(f, u)
                with act.Fori(0, (UNITS - 6) // 4) as it:
                    for u in range(4, 8):
                        unit(f, u, it)
                for u in range(UNITS - 2, UNITS):
                    unit(f, u)
                if f == 0:
                    for k in range(POOL_UNITS):
                        act.wait_ge(d_scaled, k + 1)
                        d_split(D_POOL + k)
                    for c in range(KT // 2):
                        act.wait_ge(u_done, c + 1)
                        act.activation(xT_hi[:, 2 * c:2 * c + 2, :], ps[:, WORK + c, :].rearrange("p (a s) -> p a s", a=2), ACT.Copy).then_inc(u_hi_done, 1)
                    channel_major(1)
                    g_split(1, RAW_UNITS)
                if f == 1:
                    channel_major(2)
                    g_split(2, RAW_UNITS)
                if f == 2:
                    g_split(None, 0)
                    g_split(None, 1)
                    channel_major(QKV_EVENT)
                    attention_act(act, g_split, d_split)
                    channel_major(4)
                    g_split(3, RAW_UNITS)

        def rotary_tables(dve, link):
            dve.wait_ge(small_in, 64)
            dve.wait_ge(consts, 1)
            turn, parts = 2.0 * math.pi, []
            for i in range(4):
                grid = 2.0 ** (9 + 11 * i)
                part = math.floor(turn * grid) / grid if i < 3 else float(np.float32(turn))
                parts.append(part)
                turn -= part
            A = [ang[:, i] for i in range(8)]
            magic = 1.5 * 2.0 ** 23
            link(dve.tensor_copy(ang[:, 7, :, 0], pos_i[:, :]))
            link(dve.tensor_tensor(A[0], ang[:, 7, :, 0:1].to_broadcast([P, TT, HALF]),
                                   invf[:, :].rearrange("p (a j) -> p a j", a=1).to_broadcast([P, TT, HALF]), ALU.mult))
            link(dve.tensor_scalar(A[2], A[0], 1.0 / (2.0 * math.pi), magic, ALU.mult, ALU.add))
            link(dve.tensor_scalar(A[2], A[2], magic, None, ALU.subtract))
            link(dve.tensor_scalar(A[3], A[2], 1.0 / 2048, magic, ALU.mult, ALU.add))
            link(dve.tensor_scalar(A[3], A[3], magic, 2048.0, ALU.subtract, ALU.mult))
            link(dve.tensor_tensor(A[2], A[2], A[3], ALU.subtract))
            for part in parts:
                for digit in (A[3], A[2]):
                    link(dve.scalar_tensor_tensor(A[0], digit, -part, A[0], ALU.mult, ALU.add))
            link(dve.tensor_scalar(A[1], A[0], math.pi / 2, None, ALU.add))
            link(dve.tensor_scalar(A[4], A[1], math.pi, -2.0 * math.pi, ALU.is_gt, ALU.mult))
            link(dve.tensor_tensor(A[1], A[1], A[4], ALU.add))
            top = 3.1415925
            link(dve.tensor_scalar(A[0], A[0], top, -top, ALU.min, ALU.max))
            dve.tensor_scalar(A[1], A[1], top, -top, ALU.min, ALU.max).then_inc(ang_done, 1)
            dve.wait_ge(sin_done, 1)
            link(dve.tensor_scalar(rot[:, :, 2, :], rot[:, :, 1, :], -1.0, None, ALU.mult))

        def attention_dve(dve, link, note, g_split, d_split):
            def rotate(v, tmp_a, tmp_b, heads, t):
                cos, sin, nsin = (rot[:, t, c, :].rearrange("p (a j) -> p a j", a=1).to_broadcast([P, heads, HALF]) for c in range(3))
                lo, hi = v[:, :, 0:HALF], v[:, :, HALF:ROT]
                dve.tensor_tensor(tmp_a[:, :, 0:HALF], lo, cos, ALU.mult)
                dve.tensor_tensor(tmp_a[:, :, HALF:ROT], hi, cos, ALU.mult)
                dve.tensor_tensor(tmp_b[:, :, 0:HALF], hi, nsin, ALU.mult)
                link(dve.tensor_tensor(tmp_b[:, :, HALF:ROT], lo, sin, ALU.mult))
                return dve.tensor_tensor(v[:, :, 0:ROT], tmp_a, tmp_b, ALU.add)

            def chunk(c, t):
                dve.wait_ge(qkv_done, 2 * c + t + 1)
                src = ps[:, (2 * c + t) % 4, :]
                if c == 0:
                    as_heads = lambda v: v.rearrange("p (g d) -> p g d", g=NKV)
                    dve.tensor_tensor(vd[:, t, :, 0, :], as_heads(src[:, 256:512]), as_heads(aux[:, 1280:1536]), ALU.add)
                    v, heads = kd[:, t, :, 0, :], NKV
                    link(dve.tensor_tensor(v, as_heads(src[:, 0:256]), as_heads(aux[:, 1024:1280]), ALU.add))
                else:
                    lo = 512 * (c - 1)
                    flat, heads = xn[:, t, lo:lo + 512], 8
                    v = flat.rearrange("p (h d) -> p h d", h=8)
                    if c == 1:
                        dve.wait_ge(ax_done, 8 + t + 1)
                    link(dve.tensor_tensor(flat, src, aux[:, lo:lo + 512], ALU.add))
                after(dve, qkv_sb, 2 * c + t)
                tmp = rtmp[:, :, 0:heads, :]
                rotate(v, tmp[:, 0], tmp[:, 1], heads, t).then_inc(qkv_sb, 1)

            def scores(i):
                g, n = TASKS[i]
                s = sc[i % 2]
                if n == 0:
                    dve.wait_ge(s_done, i + 1)
                    after(dve, pT_ps, i - 1)
                    ins = dve.tensor_tensor(s[:, :, :], ps[:, WORK, :].rearrange("p (h j) -> p h j", h=4),
                                            cst[:, 1:2, :].to_broadcast([P, 4, P]), ALU.add)
                else:
                    dve.wait_ge(diag_done, g + 1)
                    ins = dve.copy_predicated(s[:, :, :], cst[:, 2:3, :].bitcast(i32).to_broadcast([P, 4, P]), two_banks[:, :, 0:P])
                ins.then_inc(s_sb, 1)
                dve.wait_ge(s_sb, i + 1)
                st = sm[:, i % 2]
                sink = sinkb[:, 4 * g:4 * g + 4]
                link(dve.tensor_reduce(st[:, 0, :], s[:, :, :], axis=AX.X, op=ALU.max))
                link(dve.scalar_tensor_tensor(st[:, 5, :], st[:, 0, :], SCALE, sink, ALU.mult, ALU.max))
                dve.tensor_tensor(st[:, 2, :], sink, st[:, 5, :], ALU.subtract)
                dve.tensor_scalar(st[:, 1, :], st[:, 5, :], -1.0, None, ALU.mult).then_inc(m_done, 1)

            def probabilities(i):
                st = sm[:, i % 2]
                dve.wait_ge(e_done, i + 1)
                link(dve.tensor_tensor(st[:, 5, :], st[:, 3, :], st[:, 4, :], ALU.add))
                link(dve.reciprocal(st[:, 0, :], st[:, 5, :]))
                dve.tensor_tensor(sc[i % 2][:, :, :], sc[i % 2][:, :, :], st[:, 0, :].rearrange("p (h a) -> p h a", a=1).to_broadcast([P, 4, P]), ALU.mult).then_inc(p_done, 1)

            def pT_masked(i):
                if TASKS[i][1] == 1:
                    dve.wait_ge(pT_ps, i + 1)
                    src = ps[:, WORK + 2, :].rearrange("p (h q) -> p h q", h=4)
                    dve.tensor_tensor(pT[i % 2][:, 1], src, cst[:, 3:4, :].to_broadcast([P, 4, P]), ALU.mult)
                    dve.tensor_tensor(pT[i % 2][:, 0], src, prevT[:, :, :].to_broadcast([P, 4, P]), ALU.mult).then_inc(pT_v, 1)

            def o_lo(i):
                g, n = TASKS[i]
                dve.wait_ge(oT_hi_done, i + 1)
                bank = ps[:, WORK + 3, :].rearrange("p (a e q) -> p a e q", a=2, e=2)
                for e, rows in enumerate((slice(0, HD), slice(HD, P))):
                    last = dve.tensor_tensor(xT_lo[rows, 2 * g:2 * g + 2, n * P:(n + 1) * P], bank[rows, :, e, :],
                                             xT_hi[rows, 2 * g:2 * g + 2, n * P:(n + 1) * P].bitcast(f32), ALU.subtract)
                last.then_inc(oT_lo_done, 1)

            dve.wait_ge(aux_in, 64)
            dve.wait_ge(x_lo_done, 4 * QKV_EVENT + 4)
            link(dve.tensor_scalar(prevT[:, 0, :], cst[:, 3, :], -1.0, 1.0, ALU.mult, ALU.add))
            chunk(0, 0)
            g_split(None, 2)
            chunk(0, 1)
            g_split(None, 3)
            d_split(D_WO)
            d_split(D_WO + 1)
            g_split(None, 4)
            chunk(1, 0)
            chunk(1, 1)
            g_split(None, 5)
            scores(0)
            for i in range(len(TASKS)):
                probabilities(i)
                if i >= 1:
                    o_lo(i - 1)
                if i + 1 < len(TASKS):
                    scores(i + 1)
                pT_masked(i)
                if i == 1:
                    chunk(2, 0)
                    chunk(2, 1)
                if i >= 2:
                    d_split(D_WO + i)
            o_lo(len(TASKS) - 1)


        @block.vector
        def _(dve):
            count = [0]

            def note(ins):
                count[0] += 1
                ins.then_inc(order, 1)
                return count[0]

            def link(ins):
                dve.wait_ge(order, note(ins))

            def g_split(f, u, it=0):
                X, G, src = split_unit(f, u)
                for half in range(2):
                    dve.wait_ge(g_hi_done, 2 * X + half + 1 + 8 * it)
                    dve.tensor_tensor(g_half(g_lo, X, half), src(G, half), g_half(g_hi, X, half).bitcast(f32), ALU.subtract).then_inc(g_lo_done, 1)

            def d_split(E, it=0):
                dve.wait_ge(d_hi_done, E + 1 + 4 * it)
                dve.tensor_tensor(d_lo[:, E % D_SLOTS, :], raw_d[:, (E // 2) % 2, E % 2, :], d_hi[:, E % D_SLOTS, :].bitcast(f32), ALU.subtract).then_inc(d_lo_done, 1)

            def h_of(f, u, it=0):
                dve.wait_ge(silu_done, UNITS * f + u + 1 + 4 * it)
                dve.tensor_tensor(hf[:, u % 2, :], silu[:, u % 2, :], ps[:, WORK + u % 2, S:2 * S], ALU.mult).then_inc(hf_done, 1)

            def h_lo_of(f, u, it=0):
                dve.wait_ge(h_hi_done, UNITS * f + u + 1 + 4 * it)
                slot = (D0[f] + u) % D_SLOTS
                dve.tensor_tensor(hT_lo[:, slot, :], hf[:, u % 2, :], hT_hi[:, slot, :].bitcast(f32), ALU.subtract).then_inc(h_lo_done, 1)

            def unit(f, u, it=0):
                h_of(f, u, it)
                if 1 <= u < UNITS - 2:
                    g_split(f, u + 2, it)
                h_lo_of(f, u, it)
                if u + 1 < UNITS:
                    d_split(D0[f] + u + 1, it)
                if f > 0 and u in (2, 3):
                    residual(FFN_EVENT[f], u - 2)

            def normalise(n, t, coef, filler=None, res=ax):
                halves = [slice(512 * h, 512 * (h + 1)) for h in range(2)]
                at = []
                for h in range(2):
                    dve.wait_ge(acc_done, 4 * n + 2 * t + h + 1)
                    at.append(note(dve.scalar_tensor_tensor(xn[:, t, halves[h]], ACC[t][h], coef, res[:, t, halves[h]], ALU.mult, ALU.add)))
                    dve.wait_ge(order, at[h])
                    last = dve.bn_stats(stats[:, h, :], xn[:, t, halves[h]])
                    if h == 0:
                        note(last)
                link(last)
                dve.bn_aggr(mv[:, t, :], stats[:, :, :].rearrange("p a b -> p (a b)")).then_inc(stat_done, 1)
                if filler:
                    filler(t)
                dve.wait_ge(rstd_done, 2 * n + t + 1)
                for h in range(2):
                    dve.tensor_scalar(xn[:, t, halves[h]], xn[:, t, halves[h]], mv[:, t, 0:1], rstd[:, t, 1:2],
                                      ALU.subtract, ALU.mult).then_inc(xn_done, 1)

            def channel_major(e, t):
                dve.wait_ge(tr_done, 4 * e + 2 * t + 1)
                bank = ps[:, WORK + 2, :].rearrange("p (k s) -> p k s", k=4)
                if e == 0:
                    last = dve.tensor_copy(xf[:, t, 0:4, :], bank)
                else:
                    for k in range(4):
                        last = dve.tensor_scalar(xf[:, t, k, :], bank[:, k, :], lnT[:, 0, e, k:k + 1], lnT[:, 1, e, k:k + 1], ALU.mult, ALU.add)
                last.then_inc(xf_lo_done, 1)

            def x_lo(e, t):
                for q in range(2):
                    dve.wait_ge(x_hi_done, 4 * e + 2 * t + q + 1)
                    at = slice(4 * q, 4 * q + 4), slice(t * P, (t + 1) * P)
                    dve.tensor_tensor(xT_lo[:, at[0], at[1]], xf[:, t, at[0], :], xT_hi[:, at[0], at[1]].bitcast(f32),
                                      ALU.subtract).then_inc(x_lo_done, 1)

            def residual(n, t):
                if t == 0:
                    dve.wait_ge(gb_in, 32 * (n + 1))
                dve.wait_ge(xn_done, 4 * n + 2 * t + 2)
                link(dve.scalar_tensor_tensor(ax[:, t, :], xn[:, t, :], ALPHA, gb[:, 0, :], ALU.mult, ALU.mult))
                dve.scalar_tensor_tensor(ax[:, t, :], gb[:, 1, :], ALPHA, ax[:, t, :], ALU.mult, ALU.add).then_inc(ax_done, 1)

            dve.wait_ge(lnT_ps, 1)
            dve.tensor_copy(lnT[:, :, :, :].rearrange("p a n k -> p (a n k)"), ps[:, 7, 0:96]).then_inc(lnT_done, 1)
            for t in range(TT):
                channel_major(0, t)
            for t in range(TT):
                x_lo(0, t)
            rotary_tables(dve, link)
            g_split(0, RAW_UNITS)
            for t in range(TT):
                dve.tensor_scalar(ax[:, t, :], xn[:, t, :], ALPHA, None, ALU.mult).then_inc(ax_done, 1)
            for f in range(FFNS):
                d_split(D0[f])
                for u in range(4):
                    unit(f, u)
                with dve.Fori(0, (UNITS - 6) // 4) as it:
                    for u in range(4, 8):
                        unit(f, u, it)
                for u in range(UNITS - 2, UNITS):
                    unit(f, u)
                if f == 0:
                    for t in range(TT):
                        normalise(0, t, 0.5, filler=lambda t: d_split(D_POOL + t))
                        residual(0, t)
                    for c in range(KT // 2):
                        dve.wait_ge(u_hi_done, c + 1)
                        dve.tensor_tensor(xT_lo[:, 2 * c:2 * c + 2, :], ps[:, WORK + c, :].rearrange("p (a s) -> p a s", a=2),
                                          xT_hi[:, 2 * c:2 * c + 2, :].bitcast(f32), ALU.subtract).then_inc(u_lo_done, 1)
                    for t in range(TT):
                        dve.wait_ge(axb_done, t + 1)
                        normalise(1, t, 1.0, res=axb)
                        channel_major(1, t)
                    for t in range(TT):
                        x_lo(1, t)
                    g_split(1, RAW_UNITS)
                elif f == 1:
                    for t in range(TT):
                        normalise(2, t, 0.5)
                        channel_major(2, t)
                    for t in range(TT):
                        x_lo(2, t)
                    g_split(2, RAW_UNITS)
                elif f == 2:
                    for t in range(TT):
                        normalise(3, t, 0.5, filler=lambda t: g_split(None, t))
                        channel_major(QKV_EVENT, t)
                        x_lo(QKV_EVENT, t)
                    attention_dve(dve, link, note, g_split, d_split)
                    for t in range(TT):
                        dve.wait_ge(ax_done, 8 + t + 1)
                        normalise(4, t, 1.0)
                        channel_major(4, t)
                    for t in range(TT):
                        x_lo(4, t)
                    g_split(3, RAW_UNITS)
                else:
                    for t in range(TT):
                        normalise(5, t, 0.5)
                        if t == 0:
                            dve.wait_ge(gb_in, 32 * 6)
                        for h in range(2):
                            dve.wait_ge(xn_done, 4 * 5 + 2 * t + h + 1)
                            y = xn[:, t, 512 * h:512 * (h + 1)]
                            link(dve.tensor_tensor(y, y, gb[:, 0, 512 * h:512 * (h + 1)], ALU.mult))
                            dve.tensor_tensor(y, y, gb[:, 1, 512 * h:512 * (h + 1)], ALU.add).then_inc(y_done, 1)

        def pool_pe(pe, three):
            pe.wait_ge(band_in, 16)
            pe.wait_ge(hf_done, UNITS)
            for t in range(TT):
                for c in range(KT // 2):
                    for k in (2 * c, 2 * c + 1):
                        b = band[:, k // 2, :]
                        o = ps[:, WORK + c, (k % 2) * S:(k % 2 + 1) * S]
                        if k == 0:
                            pe.wait_ge(ax_done, 3 + t)
                        if t == 0:
                            last = pe.matmul(o, ax[:, 0, k * P:(k + 1) * P], b[:, 0:S], start=k % 2 == 0, stop=False)
                            if k == 0:
                                last.then_inc(d_used, 1)
                        else:
                            last = pe.matmul(o[:, P:S], ax[:, 1, k * P:(k + 1) * P], b[:, S:S + P], start=False, stop=k % 2 == 1)
                    if t == 1:
                        last.then_inc(u_done, 1)
            for t in range(TT):
                for g in range(len(WINDOWS)):
                    for j in range(2):
                        k, E = 2 * g + j, D_POOL + j
                        if t == 0:
                            pe.wait_ge(u_lo_done, g + 1)
                            if g == 0:
                                pe.wait_ge(d_lo_done, E + 1)
                        tok = slice(t * P, (t + 1) * P)
                        w_hi, w_lo = (b[:, E % D_SLOTS, g * GC:(g + 1) * GC] for b in (d_hi, d_lo))
                        last = three(ACC[t][g // 2][:, (g % 2) * GC:(g % 2 + 1) * GC], xT_hi[:, k, tok], xT_lo[:, k, tok],
                                     w_hi, w_lo, j == 0, j == 1)
                    if g % 2 == 1:
                        last.then_inc(acc_done, 1)

        def attention_pe(pe, three, down, transposes):
            ident = cst[:, 0, :]
            e = QKV_EVENT

            def qkv(c, half, t, used=False):
                X = X_QKV + 2 * c + half
                bank = ps[:, (2 * c + t) % 4, :]
                if t == 0:
                    pe.wait_ge(g_lo_done, 2 * X + 2)
                if c == 0:
                    pe.wait_ge(x_lo_done, 4 * e + 2 * t + half + 1)
                if c == 2 and half == 0:
                    pe.wait_ge(qkv_sb, t + 1)
                tok = slice(t * P, (t + 1) * P)
                for j in range(4):
                    w_hi, w_lo = (b[:, X % G_SLOTS, 512 * j:512 * (j + 1)] for b in (g_hi, g_lo))
                    k = 4 * half + j
                    x_hi, x_lo = xT_hi[:, k, tok], xT_lo[:, k, tok]
                    ins = pe.matmul(bank, x_hi, w_hi, start=k == 0, stop=False)
                    if j == 0 and used:
                        ins.then_inc(g_used, 1)
                    pe.matmul(bank, x_hi, w_lo, start=False, stop=False)
                    last = pe.matmul(bank, x_lo, w_hi, start=False, stop=k == KT - 1)
                return last

            def to_channels(c, t, used=False):
                if c == 0:
                    pe.wait_ge(dup_done, t + 1)
                    pe.wait_ge((xf_lo_done, xf_up_done)[t], 2 * e + 2)
                else:
                    pe.wait_ge(qkv_sb, 2 * c + t + 1)
                    if c == 1:
                        pe.wait_ge(qkT_done, t + 1)
                for j in range(4):
                    src = kd[:, t, j, :, :].rearrange("p e d -> p (e d)") if c == 0 else xn[:, t, 512 * (c - 1) + P * j:512 * (c - 1) + P * (j + 1)]
                    last = pe.transpose(ps[:, (2 if c == 2 else WORK + 2) + t, P * j:P * (j + 1)], src, ident)
                    if j == 0 and used:
                        last.then_inc(g_used, 1)
                last.then_inc(qkT_ps, 1)

            def scores(i):
                g, n = TASKS[i]
                if i == 0:
                    pe.wait_ge(hf_done, 3 * UNITS)
                if i in (0, 1, 4):
                    pe.wait_ge(qkT_done, {0: 3, 1: 4, 4: 6}[i])
                after(pe, s_sb, i)
                for h in range(4):
                    head = 4 * g + h
                    keys = slice(0, (n + 1) * P)
                    o = ps[:, WORK, P * h:P * (h + 1)] if n == 0 else two_banks[:, h, :]
                    last = pe.matmul(o, qT[:, head // 2, n * P:(n + 1) * P], kT[:, g, head % 2, keys], start=True, stop=True)
                last.then_inc(s_done, 1)

            def probs_T(i):
                if i == 0:
                    pe.wait_ge(qkT_done, 3)
                pe.wait_ge(p_done, i + 1)
                for h in range(4):
                    last = pe.transpose(ps[:, WORK + 2, P * h:P * (h + 1)], sc[i % 2][:, h, :], ident)
                last.then_inc(pT_ps, 1)

            def values(i):
                g, n = TASKS[i]
                pe.wait_ge(pT_a if n == 0 else pT_v, g + 1)
                after(pe, oT_lo_done, i)
                o = ps[:, WORK + 3, :]
                own = pT[i % 2][:, 1].rearrange("p h q -> p (h q)")
                prev = pT[i % 2][:, 0].rearrange("p h q -> p (h q)")
                v = [vd[:, t, g, :, :].rearrange("p e d -> p (e d)") for t in range(TT)]
                if i == 0:
                    pe.wait_ge(qkT_done, 4)
                if n == 1:
                    ins = pe.matmul(o, v[0], prev, start=True, stop=False)
                    if i == 1:
                        ins.then_inc(g_used, 1)
                pe.matmul(o, v[n], own, start=n == 0, stop=True).then_inc(oT_ps, 1)

            def wo(k, ts=(0, 1)):
                if ts[0] == 0:
                    pe.wait_ge(oT_lo_done, 2 * (k // 2) + (2 if ts[-1] == 1 else 1))
                    if k == 0:
                        pe.wait_ge(qkT_done, 6)
                else:
                    pe.wait_ge(oT_lo_done, 2 * (k // 2) + 2)
                down(D_WO + k, xT_hi[:, k, :], xT_lo[:, k, :], ts, k == 0, k == WO_UNITS - 1)

            transposes(e, 0, used=1)
            qkv(0, 0, 0)
            qkv(0, 1, 0).then_inc(qkv_done, 1)
            transposes(e, 1)
            qkv(0, 0, 1).then_inc(g_used, 1)
            qkv(0, 1, 1).then_inc(qkv_done, 1)
            qkv(1, 0, 0, used=True)
            qkv(1, 0, 1).then_inc(g_used, 1)
            qkv(1, 1, 0).then_inc(qkv_done, 1)
            to_channels(0, 0)
            qkv(1, 1, 1).then_inc(qkv_done, 1)
            to_channels(0, 1, used=True)
            to_channels(1, 0)
            qkv(2, 0, 0)
            scores(0)
            to_channels(1, 1)
            qkv(2, 0, 1).then_inc(g_used, 1)
            for i in range(len(TASKS)):
                if i + 1 < len(TASKS):
                    scores(i + 1)
                if i == 2:
                    to_channels(2, 0)
                    to_channels(2, 1)
                probs_T(i)
                if i < 2:
                    qkv(2, 1, i).then_inc(qkv_done, 1)
                else:
                    wo(i - 2, (0, 1) if i < 6 else (0,))
                values(i)
            wo(6, (0,))
            wo(7, (0,))
            for k in range(4, 8):
                wo(k, (1,))

        @block.tensor
        def _(pe):
            ident = cst[:, 0, :]

            def three(out_, l_hi, l_lo, r_hi, r_lo, start, stop):
                pe.matmul(out_, l_hi, r_hi, start=start, stop=False)
                pe.matmul(out_, l_hi, r_lo, start=False, stop=False)
                return pe.matmul(out_, l_lo, r_hi, start=False, stop=stop)

            def gate_up_raw(f, u, t):
                e, G = FFN_EVENT[f], G0[f] + u
                if u == 0 and t == 0:
                    pe.wait_ge(g_in[(G // 2) % 2], 32 * (G // 4 + 1))
                for m in range(2):
                    for k in range(KT):
                        if m == 0 and k % 4 == 0:
                            pe.wait_ge((xf_lo_done, xf_up_done)[k // 4], 2 * e + t + 1)
                        last = pe.matmul(ps[:, WORK + u % 2, m * S + t * P:m * S + (t + 1) * P], raw_unit(G, m)[:, k, :],
                                         xf[:, t, k, :], start=k == 0, stop=k == KT - 1)
                if t == TT - 1:
                    last.then_inc(g_used, 1)

            def gate_up(f, u, it=0):
                X = X0[f] + u
                pe.wait_ge(g_lo_done, 2 * X + 2 + 8 * it)
                pe.wait_ge(hf_done, UNITS * f + u - 1 + 4 * it)
                for m in range(2):
                    for k in range(KT):
                        if u == RAW_UNITS and m == 0 and k == 0:
                            pe.wait_ge(x_lo_done, 4 * FFN_EVENT[f] + 4)
                        w_hi, w_lo = g_half(g_hi, X, m)[:, k, :], g_half(g_lo, X, m)[:, k, :]
                        last = three(ps[:, WORK + u % 2, m * S:(m + 1) * S], w_hi, w_lo,
                                     xT_hi[:, k, :], xT_lo[:, k, :], k == 0, k == KT - 1)
                last.then_inc(g_used, 1)

            def down(E, l_hi, l_lo, ts, first, final, it=0):
                if ts[0] == 0:
                    pe.wait_ge(d_lo_done, E + 1 + 4 * it)
                for t in ts:
                    for h in range(2):
                        w_hi, w_lo = (b[:, E % D_SLOTS, 512 * h:512 * (h + 1)] for b in (d_hi, d_lo))
                        tok = slice(t * P, (t + 1) * P)
                        last = three(ACC[t][h], l_hi[:, tok], l_lo[:, tok], w_hi, w_lo, first, final)
                        if final:
                            last.then_inc(acc_done, 1)
                if not final and ts[-1] == TT - 1:
                    last.then_inc(d_used, 1)

            def ffn_down(f, u, ts=(0, 1), it=0):
                if ts[0] == 0:
                    pe.wait_ge(h_lo_done, UNITS * f + u + 1 + 4 * it)
                E = D0[f] + u
                final = u == UNITS - 1
                down(E, hT_hi[:, E % D_SLOTS, :], hT_lo[:, E % D_SLOTS, :], ts, u == 0, final, it)

            def transposes(e, t, used=0):
                for q in range(2):
                    pe.wait_ge(*((xn_done, 4 * e + 2 * t + q + 1) if e > 0 else (x_in[t], 16)))
                    after(pe, (xf_lo_done, xf_up_done)[q], 2 * e + t)
                    for k in range(4 * q, 4 * q + 4):
                        last = pe.transpose(ps[:, WORK + 2 + q, (k % 4) * P:(k % 4 + 1) * P], xn[:, t, k * P:(k + 1) * P], ident)
                        if k == 0 and used:
                            last.then_inc(d_used, used)
                    last.then_inc(tr_done, 1)

            pe.wait_ge(cst_in, 16)
            pe.wait_ge(small_in, 64)
            for a in range(2):
                last = pe.transpose(ps[:, 7, 48 * a:48 * (a + 1)], lnrow[:, a, :], ident[0:48, 0:48])
            last.then_inc(lnT_ps, 1)
            pe.wait_ge(lnT_done, 1)
            for f in range(FFNS):
                e = FFN_EVENT[f]
                transposes(e, 0, used=(0, 2, 1, 1)[f])
                gate_up_raw(f, 0, 0)
                transposes(e, 1)
                gate_up_raw(f, 1, 0)
                gate_up_raw(f, 0, 1)
                gate_up_raw(f, 1, 1)
                ffn_down(f, 0)
                with pe.Fori(0, (UNITS - 6) // 4) as it:
                    for u in range(2, 6):
                        gate_up(f, u, it)
                        ffn_down(f, u - 1, it=it)
                last_u = UNITS - 4
                gate_up(f, last_u)
                ffn_down(f, last_u - 1)
                gate_up(f, last_u + 1)
                ffn_down(f, last_u, (0,))
                gate_up(f, last_u + 2)
                ffn_down(f, last_u + 1, (0,))
                gate_up(f, last_u + 3)
                ffn_down(f, last_u + 2, (0,))
                ffn_down(f, last_u, (1,))
                ffn_down(f, last_u + 3, (0,))
                ffn_down(f, last_u + 1, (1,))
                ffn_down(f, last_u + 2, (1,))
                ffn_down(f, last_u + 3, (1,))
                if f == 0:
                    pool_pe(pe, three)
                if f == 2:
                    attention_pe(pe, three, down, transposes)

_INS = ["x", "positions", "ln_g", "ln_b", "ffn_w_gate", "ffn_w_up", "ffn_w_down", "pool_w", "pool_b", "pool_scale",
        "attn_w_qkv", "attn_b_qkv", "attn_sinks", "attn_w_o", "attn_b_o"]


def pool_bands():
    full = np.zeros((4, S, S), np.float64)
    for g, win in enumerate(WINDOWS):
        for s in range(S):
            lo = max(s + 1 - win, 0)
            full[g, lo:s + 1, s] = 1.0 / (s + 1 - lo)
            full[g, s, s] -= 1.0
    full /= ALPHA
    return np.concatenate([full[:, :P, :], full[:, P:, P:]], axis=2).astype(np.float32)


def attention_masks():
    q, j = np.arange(P)[:, None], np.arange(P)[None, :]
    eye = (q == j)
    return np.stack([eye, (j > q) * NEG, j > q, j >= q]).astype(np.float32)


def kernel(**inputs):
    import concourse.bacc as bacc
    from concourse.bass_utils import run_bass_kernel_spmd

    nc = bacc.Bacc("TRN2", target_bir_lowering=False, num_devices=1)
    arrays, args = {}, []
    named = [(n, inputs[n]) for n in _INS] + [("bands", pool_bands()), ("masks", attention_masks())]
    for name, a in named:
        a = np.ascontiguousarray(a)
        arrays[f"in_{name}"] = a
        args.append(nc.dram_tensor(f"in_{name}", a.shape, mybir.dt.from_np(a.dtype), kind="ExternalInput").ap())
    args.append(nc.dram_tensor("out_y", (1, S, D), mybir.dt.float32, kind="ExternalOutput").ap())
    trunk_kernel(nc, *args)
    r = run_bass_kernel_spmd(nc, [arrays], core_ids=[0])
    return r.results[0]["out_y"]
```

```python
import math
from contextlib import ExitStack

import numpy as np

import concourse.bass as bass
from concourse import mybir

P = 128
D = 1024
S = 256
F = 2816
KT = D // P
TT = S // P
UNITS = F // P
FFNS = 4
HD = 64
NQ = 16
NKV = 4
ROT = 16
HALF = ROT // 2
THETA = 500000.0
WINDOWS = (2, 4, 8, 16)
GC = D // len(WINDOWS)
ALPHA = 4.0 ** 0.25
EPS = 1e-5
SCALE = HD ** -0.5
NEG = -1e30
LAST = 3

QKV_UNITS = 6
POOL_UNITS = 2
WO_UNITS = 8
RAW_UNITS = 2
G0 = [0, UNITS, 2 * UNITS, 3 * UNITS + QKV_UNITS]
D0 = [0, UNITS + POOL_UNITS, 2 * UNITS + POOL_UNITS, 3 * UNITS + POOL_UNITS + WO_UNITS]
G_QKV = 3 * UNITS
D_POOL = UNITS
D_WO = 3 * UNITS + POOL_UNITS
X0 = [-2, UNITS - 4, 2 * UNITS - 6, 3 * UNITS - 8 + QKV_UNITS]
X_QKV = 3 * (UNITS - RAW_UNITS)
G_SLOTS = 2
D_SLOTS = 4

T_EVENT = {1: 1, 2: 2, 3: 3, 4: 4}
FFN_NORM = [0, 2, 3, 5]
FFN_EVENT = [0, 1, 2, 4]
QKV_EVENT = 3


def trunk_kernel(nc, x, positions, ln_g, ln_b, w_gate, w_up, w_down, pool_w, pool_b, pool_scale,
                 w_qkv, b_qkv, sinks, w_o, b_o, bands, masks, out):
    f32 = mybir.dt.float32
    f32r = mybir.dt.float32r
    i32 = mybir.dt.int32
    ALU = mybir.AluOpType
    ACT = mybir.ActivationFunctionType
    AX = mybir.AxisListType

    with ExitStack() as ctx:
        def sb(name, shape, dt=f32):
            return ctx.enter_context(nc.sbuf_tensor(name, shape, dt))

        def sem(name):
            return ctx.enter_context(nc.semaphore(name))

        raw_g = sb("raw_g", [P, 2, 2, 2048])
        raw_d = sb("raw_d", [P, 2, 2, 1024])
        g_hi = sb("g_hi", [P, G_SLOTS, 2048], f32r)
        g_lo = sb("g_lo", [P, G_SLOTS, 2048], f32r)
        d_hi = sb("d_hi", [P, D_SLOTS, 1024], f32r)
        d_lo = sb("d_lo", [P, D_SLOTS, 1024], f32r)
        xT_hi = sb("xT_hi", [P, KT, S], f32r)
        xT_lo = sb("xT_lo", [P, KT, S], f32r)
        hT_hi = sb("hT_hi", [P, D_SLOTS, S], f32r)
        hT_lo = sb("hT_lo", [P, D_SLOTS, S], f32r)
        xn = sb("xn", [P, TT, D])
        ax = sb("ax", [P, TT, D])
        xf = sb("xf", [P, TT, KT, P])
        silu = sb("silu", [P, 2, S])
        hf = sb("hf", [P, 2, S])
        gb = sb("gb", [P, 2, D])
        aux = sb("aux", [P, 2560])
        cst = sb("cst", [P, 4, P])
        lnT = sb("lnT", [P, 2, 6, KT])
        lnrow = ax[0:6 * KT, 1, 0:2 * P].rearrange("p (a c) -> p a c", a=2)
        stats = sb("stats", [P, 2, 6])
        mv = sb("mv", [P, 2, 2])
        rstd = sb("rstd", [P, 2, 2])
        mhalf = sb("mhalf", [P, 1])
        pos_i = sb("pos_i", [P, TT], i32)
        ang = sb("ang", [P, 8, TT, HALF])
        invf = sb("invf", [P, HALF])
        rot = sb("rot", [P, TT, 3, HALF])
        sinkb = sb("sinkb", [P, NQ])
        sm = sb("sm", [P, 2, 6, 4])
        vd = sb("vd", [P, TT, NKV, 2, HD])
        qT = sb("qT", [P, KT, S])
        kT = sb("kT", [P, NKV, 2, S])
        band = qT[:, :, :].rearrange("p k s -> p (k s)")[:, 0:4 * 384].rearrange("p (g c) -> p g c", g=4)
        kd = xf[:, 0].rearrange("p k s -> p (k s)").rearrange("p (t g e d) -> p t g e d", t=TT, g=NKV, e=2)
        sc = [silu[:, :, :].rearrange("p a s -> p (a s)").rearrange("p (h j) -> p h j", h=4),
              hf[:, :, :].rearrange("p a s -> p (a s)").rearrange("p (h j) -> p h j", h=4)]
        pT = [gb[:, i, :].rearrange("p (b h q) -> p b h q", b=2, h=4) for i in range(2)]

        ps = ctx.enter_context(nc.psum_tensor("ps", [P, 8, 512], f32))
        ACC = [[ps[:, 2 * t + h, :] for h in range(2)] for t in range(TT)]
        WORK = 4

        g_in = [sem("g_in0"), sem("g_in1")]
        unit0_in = [sem("unit0_gate_in"), sem("unit0_up_in"), sem("unit0_down_in")]
        d_in = [sem("d_in0"), sem("d_in1")]
        g_hi_done = sem("g_hi_done")
        g_lo_done = sem("g_lo_done")
        d_hi_done = sem("d_hi_done")
        d_lo_done = sem("d_lo_done")
        d_scaled = sem("d_scaled")
        g_used = sem("g_used")
        d_used = sem("d_used")
        silu_done = sem("silu_done")
        hf_done = sem("hf_done")
        h_hi_done = sem("h_hi_done")
        h_lo_done = sem("h_lo_done")
        acc_done = sem("acc_done")
        stat_done = sem("stat_done")
        var_done = sem("var_done")
        rstd_done = sem("rstd_done")
        xn_done = sem("xn_done")
        tr_done = sem("tr_done")
        xf_lo_done = sem("xf_lo_done")
        xf_up_done = sem("xf_up_done")
        x_hi_done = sem("x_hi_done")
        x_lo_done = sem("x_lo_done")
        ax_done = sem("ax_done")
        u_done = sem("u_done")
        u_hi_done = sem("u_hi_done")
        u_lo_done = sem("u_lo_done")
        res_step = sem("res_step")
        bs_done = sem("bs_done")
        x_in = [sem("x_in0"), sem("x_in1")]
        small_in = sem("small_in")
        band_in = sem("band_in")
        gb_in = sem("gb_in")
        aux_in = sem("aux_in")
        ident_in = sem("ident_in")
        cst_in = sem("cst_in")
        consts = sem("consts")
        lnT_ps = sem("lnT_ps")
        lnT_done = sem("lnT_done")
        kz_done = sem("kz_done")
        ang_done = sem("ang_done")
        sin_done = sem("sin_done")
        order = sem("dve_order")
        qkv_done = sem("qkv_done")
        qkv_sb = sem("qkv_sb")
        dup_done = sem("dup_done")
        qkT_ps = sem("qkT_ps")
        qkT_done = sem("qkT_done")
        s_done = sem("s_done")
        diag_done = sem("diag_done")
        s_sb = sem("s_sb")
        m_done = sem("m_done")
        e_done = sem("e_done")
        p_done = sem("p_done")
        pT_ps = sem("pT_ps")
        pT_a = sem("pT_a")
        pT_v = sem("pT_v")
        oT_ps = sem("oT_ps")
        oT_hi_done = sem("oT_hi_done")
        oT_lo_done = sem("oT_lo_done")
        y_done = sem("y_done")
        out_done = sem("out_done")

        TASKS = [(g, n) for g in range(NKV) for n in range(TT)]

        def after(eng, s, value):
            if not isinstance(value, int) or value > 0:
                eng.wait_ge(s, value)

        def raw_unit(G, half):
            c = raw_g[:, (G // 2) % 2, half, :].rearrange("p (k f) -> p k f", k=KT)
            return c[:, :, (G % 2) * P:(G % 2 + 1) * P]

        def raw_qkv(G, half):
            return raw_g[:, (G // 2) % 2, G % 2, half * 1024:(half + 1) * 1024].rearrange("p (k f) -> p k f", k=KT)

        def g_half(buf, X, half):
            return buf[:, X % G_SLOTS, half * 1024:(half + 1) * 1024].rearrange("p (k f) -> p k f", k=KT)

        def split_unit(f, u):
            return (X_QKV + u, G_QKV + u, raw_qkv) if f is None else (X0[f] + u, G0[f] + u, raw_unit)

        two_banks = ps[:, WORK:WORK + 2, :].rearrange("p b (h j) -> p (b h) j", h=2)
        rtmp = xf[:, 1, 0:2, :].rearrange("p a (h j) -> p a h j", h=8)
        prevT = xf[:, 1, 2:3, :]

        block = ctx.enter_context(nc.Block())

        @block.sync
        def _(sp):
            gate_v = w_gate.rearrange("l i (k p) f -> (l i) p k f", p=P)
            up_v = w_up.rearrange("l i (k p) f -> (l i) p k f", p=P)
            down_v = w_down.rearrange("l i (u p) d -> (l i) p u d", p=P)
            qkv_v = w_qkv[0].rearrange("(k p) c -> p k c", p=P)
            wo_v = w_o[0].rearrange("(u p) d -> p u d", p=P)
            pool_v = pool_w[0].rearrange("g (k p) d -> p k g d", p=P)

            def load_gate_up(f, c, it=0):
                C = G0[f] // 2 + c
                if c == 2:
                    sp.wait_ge(g_used, G0[f] + RAW_UNITS)
                elif c > 2:
                    sp.wait_ge(g_lo_done, 2 * (X0[f] + 2 * c - 2) + 8 * it)
                elif f > 0:
                    sp.wait_ge(g_lo_done, 2 * (X0[f] + 2 * c))
                dst = raw_g[:, C % 2, :, :].rearrange("p m (k f) -> p m k f", k=KT)
                for m, w in enumerate((gate_v, up_v)):
                    sp.dma_start(dst[:, m], w[f, :, :, bass.ds(2 * P * c + 4 * P * it, 2 * P)]).then_inc(g_in[C % 2], 16)

            def load_down(f, c, it=0):
                E = D0[f] // 2 + c
                after(sp, d_lo_done, 2 * (E - 1) + 4 * it)
                for m in range(2):
                    sp.dma_start(raw_d[:, E % 2, m, :], down_v[f, :, bass.ds(2 * c + m + 4 * it, 1), :].rearrange("p a d -> p (a d)")).then_inc(d_in[E % 2], 16)

            def load_d(E, srcs):
                after(sp, d_lo_done, 2 * (E - 1))
                for m, src in enumerate(srcs):
                    dst = raw_d[:, E % 2, m, :]
                    sp.dma_start(dst.rearrange("p (g d) -> p g d", g=4) if len(src.shape) == 3 else dst, src).then_inc(d_in[E % 2], 16)

            first = raw_g[:, 0, :, :].rearrange("p m (k f) -> p m k f", k=KT)
            for t in range(TT):
                sp.dma_start(xn[:, t, :], x[0, t * P:(t + 1) * P, :]).then_inc(x_in[t], 16)
                for m, w in enumerate((gate_v, up_v)):
                    sp.dma_start(first[:, m, :, t * P:(t + 1) * P], w[0, :, :, t * P:(t + 1) * P]).then_inc(unit0_in[m] if t == 0 else g_in[0], 16)
            sp.dma_start(raw_d[:, 0, 0, :], down_v[0, :, 0, :]).then_inc(unit0_in[2], 16)
            load_gate_up(0, 1)
            for h in range(2):
                sp.dma_start(raw_d[:, 0, 1, 512 * h:512 * (h + 1)], down_v[0, :, 1, 512 * h:512 * (h + 1)]).then_inc(d_in[0], 16)
            load_down(0, 1)
            for f in range(FFNS):
                for c in range(2 if f == 0 else 0, 3):
                    load_gate_up(f, c)
                    load_down(f, c)
                with sp.Fori(0, (UNITS // 2 - 3) // 2) as it:
                    for c in range(3, 5):
                        load_gate_up(f, c, it)
                        load_down(f, c, it)
                if f == 0:
                    load_d(D_POOL // 2, [pool_v[:, k] for k in range(2)])
                if f == 2:
                    for i, j in enumerate((2, 0, 1)):
                        C = G_QKV // 2 + i
                        sp.wait_ge(g_lo_done, 2 * (X_QKV - 2 + 2 * i))
                        for m in range(2):
                            sp.dma_start(raw_g[:, C % 2, m, :].rearrange("p (k c) -> p k c", k=4),
                                         qkv_v[:, 4 * m:4 * m + 4, 512 * j:512 * (j + 1)]).then_inc(g_in[C % 2], 16)
                        if i < 2:
                            load_d(D_WO // 2 + i, [wo_v[:, 2 * i + m] for m in range(2)])
                    for i in range(2, 4):
                        load_d(D_WO // 2 + i, [wo_v[:, 2 * i + m] for m in range(2)])
            for t in range(TT):
                for h in range(2):
                    sp.wait_ge(y_done, 2 * t + h + 1)
                    sp.dma_start(out[0, t * P:(t + 1) * P, 512 * h:512 * (h + 1)], xn[:, t, 512 * h:512 * (h + 1)]).then_inc(out_done, 16)
            sp.wait_ge(out_done, 64)

        @block.gpsimd
        def _(gp):
            for j in range(HALF):
                gp.memset(invf[:, j:j + 1], float(np.float32(THETA) ** np.float32(-2.0 * j / ROT)))
            gp.memset(mhalf[:, :], -0.5).then_inc(consts, 1)
            gp.memset(kT[:, :, :, :], 0.0).then_inc(kz_done, 1)
            gp.wait_ge(g_used, 4)
            gp.dma_start(band[:, :, :], bands.rearrange("g p c -> p g c")).then_inc(band_in, 16)
            gp.dma_start(aux[:, 0:D], pool_scale[0:1, :].to_broadcast([P, D])).then_inc(aux_in, 16)
            gp.dma_start(aux[:, D:2 * D], pool_b[0:1, :].to_broadcast([P, D])).then_inc(aux_in, 16)
            gp.wait_ge(aux_in, 32)
            gp.tensor_tensor(aux[:, D:2 * D], aux[:, D:2 * D], aux[:, 0:D], ALU.mult).then_inc(bs_done, 1)

            def residual_mult(n, t):
                gp.wait_ge(xn_done, 4 * n + 2 * t + 2)
                gp.tensor_tensor(ax[:, t, :], xn[:, t, :], gb[:, 0, :], ALU.mult).then_inc(res_step, 1)

            def residual_add(step, t):
                gp.wait_ge(res_step, step + 3 + t)
                gp.tensor_tensor(ax[:, t, :], ax[:, t, :], gb[:, 1, :], ALU.add).then_inc(ax_done, 1)

            for n in range(6):
                if n > 0:
                    gp.wait_ge(ax_done, 2 * n + 2)
                if n == 4:
                    gp.wait_ge(oT_ps, len(TASKS))
                gp.dma_start(gb[:, 0, :], ln_g[n // 3, n % 3:n % 3 + 1, :].to_broadcast([P, D])).then_inc(gb_in, 16)
                gp.dma_start(gb[:, 1, :], ln_b[n // 3, n % 3:n % 3 + 1, :].to_broadcast([P, D])).then_inc(gb_in, 16)
                if n == 0:
                    for k in range(POOL_UNITS):
                        raw = raw_d[:, (D_POOL // 2) % 2, k, :]
                        if k == 0:
                            gp.wait_ge(d_in[(D_POOL // 2) % 2], 32 * (D_POOL // 4 + 1))
                        gp.tensor_tensor(raw, raw, aux[:, 0:D], ALU.mult).then_inc(d_scaled, 1)
                    gp.wait_ge(bs_done, 1)
                step = {0: 0, 3: 4}.get(n)
                if step is not None:
                    gp.wait_ge(gb_in, 32 * (n + 1))
                    gp.tensor_scalar(gb[:, :, :], gb[:, :, :], ALPHA, None, ALU.mult).then_inc(res_step, 1)
                    gp.wait_ge(res_step, step + 1)
                    if n == 3:
                        gp.wait_ge(aux_in, 64)
                    gp.tensor_tensor(gb[:, 1, :], gb[:, 1, :], aux[:, D:2 * D] if n == 0 else aux[:, 1536:2560], ALU.add).then_inc(res_step, 1)
                    gp.wait_ge(res_step, step + 2)
                if n == 3:
                    X, G, src = split_unit(None, 1)
                    gp.wait_ge(g_hi_done, 2 * X + 1)
                    gp.wait_ge(g_lo_done, 2 * X)
                    gp.tensor_tensor(g_half(g_lo, X, 0), src(G, 0), g_half(g_hi, X, 0).bitcast(f32), ALU.subtract).then_inc(g_lo_done, 1)
                for t in range(TT):
                    gp.wait_ge(stat_done, 2 * n + t + 1)
                    gp.tensor_scalar(rstd[:, t, 0:1], mv[:, t, 1:2], EPS, None, ALU.add).then_inc(var_done, 1)
                    gp.wait_ge(var_done, 2 * n + t + 1)
                    gp.tensor_tensor(rstd[:, t, 1:2], rstd[:, t, 0:1], mhalf[:, :], ALU.pow).then_inc(rstd_done, 1)
                    if step is not None and t == 0:
                        residual_mult(n, 0)
                if step is not None:
                    residual_add(step, 0)
                    residual_mult(n, 1)
                    residual_add(step, 1)
                if n == 1:
                    gp.dma_start(aux[:, 0:1536], b_qkv[0:1, :].to_broadcast([P, 1536])).then_inc(aux_in, 16)
                    gp.dma_start(aux[:, 1536:2560], b_o[0:1, :].to_broadcast([P, D])).then_inc(aux_in, 16)

        def attention_act(act, g_split, d_split):
            def wo_split(k):
                d_split(D_WO + k)

            def duplicate(t):
                act.wait_ge(qkv_sb, t + 1)
                act.activation(kd[:, t, :, 1, :], kd[:, t, :, 0, :], ACT.Copy)
                act.activation(vd[:, t, :, 1, :], vd[:, t, :, 0, :], ACT.Copy).then_inc(dup_done, 1)

            def transposed(c, t):
                act.wait_ge(qkT_ps, 2 * c + t + 1)
                bank = ps[:, (2 if c == 2 else WORK + 2) + t, :].rearrange("p (a s) -> p a s", a=4)
                if c == 0:
                    if t == 0:
                        act.wait_ge(kz_done, 1)
                    act.activation(kT[0:HD, :, 0, t * P:(t + 1) * P], bank[0:HD], ACT.Copy)
                    act.activation(kT[HD:P, :, 1, t * P:(t + 1) * P], bank[HD:P], ACT.Copy).then_inc(qkT_done, 1)
                else:
                    act.activation(qT[:, 4 * c - 4:4 * c, t * P:(t + 1) * P], bank, ACT.Copy).then_inc(qkT_done, 1)

            def diag(i):
                g, n = TASKS[i]
                if n == 1:
                    act.wait_ge(s_done, i + 1)
                    after(act, pT_ps, i - 1)
                    act.activation(sc[i % 2][:, :, :], two_banks[:, :, P:2 * P], ACT.Copy).then_inc(diag_done, 1)

            def exps(i):
                act.wait_ge(m_done, i + 1)
                for h in range(4):
                    act.activation(sc[i % 2][:, h, :], sc[i % 2][:, h, :], ACT.Exp, bias=sm[:, i % 2, 1, h:h + 1],
                                   scale=SCALE, accum_out=sm[:, i % 2, 3, h:h + 1])
                act.activation(sm[:, i % 2, 4, :], sm[:, i % 2, 2, :], ACT.Exp).then_inc(e_done, 1)

            def pT_copy(i):
                if TASKS[i][1] == 0:
                    act.wait_ge(pT_ps, i + 1)
                    if i == 0:
                        act.wait_ge(ax_done, 10)
                    act.activation(pT[i % 2][:, 1], ps[:, WORK + 2, :].rearrange("p (h q) -> p h q", h=4), ACT.Copy).then_inc(pT_a, 1)

            def o_hi(i):
                g, n = TASKS[i]
                act.wait_ge(oT_ps, i + 1)
                bank = ps[:, WORK + 3, :].rearrange("p (a e q) -> p a e q", a=2, e=2)
                act.activation(xT_hi[0:HD, 2 * g:2 * g + 2, n * P:(n + 1) * P], bank[0:HD, :, 0, :], ACT.Copy)
                act.activation(xT_hi[HD:P, 2 * g:2 * g + 2, n * P:(n + 1) * P], bank[HD:P, :, 1, :], ACT.Copy).then_inc(oT_hi_done, 1)

            g_split(None, 2)
            duplicate(0)
            g_split(None, 3)
            duplicate(1)
            wo_split(0)
            wo_split(1)
            g_split(None, 4)
            transposed(0, 0)
            transposed(0, 1)
            transposed(1, 0)
            g_split(None, 5)
            transposed(1, 1)
            exps(0)
            for i in range(len(TASKS)):
                if i >= 1:
                    o_hi(i - 1)
                if i >= 2:
                    wo_split(i)
                if i == 2:
                    transposed(2, 0)
                    transposed(2, 1)
                if i + 1 < len(TASKS):
                    diag(i + 1)
                pT_copy(i)
                if i + 1 < len(TASKS):
                    exps(i + 1)
            o_hi(len(TASKS) - 1)

        @block.scalar
        def _(act):
            def g_split(f, u, it=0):
                X, G, src = split_unit(f, u)
                act.wait_ge(g_in[(G // 2) % 2], 32 * (G // 4 + 1) + 32 * it)
                after(act, g_used, (G0[f] + u - 3 if f is not None and u < 4 else G - 1) + 4 * it)
                for half in range(2):
                    act.activation(g_half(g_hi, X, half), src(G, half), ACT.Copy).then_inc(g_hi_done, 1)

            def d_split(E, it=0):
                if E == 0:
                    act.wait_ge(unit0_in[2], 16)
                else:
                    act.wait_ge(d_in[(E // 2) % 2], 32 * (E // 4 + 1) + 32 * it)
                after(act, d_used, E - D_SLOTS + 1 + 4 * it)
                act.activation(d_hi[:, E % D_SLOTS, :], raw_d[:, (E // 2) % 2, E % 2, :], ACT.Copy).then_inc(d_hi_done, 1)

            def silu_of(f, u, it=0):
                act.wait_ge(g_used, G0[f] + u + 1 + 4 * it)
                act.activation(silu[:, u % 2, :], ps[:, WORK + u % 2, 0:S], ACT.Silu).then_inc(silu_done, 1)

            def h_hi_of(f, u, it=0):
                act.wait_ge(hf_done, UNITS * f + u + 1 + 4 * it)
                act.activation(hT_hi[:, (D0[f] + u) % D_SLOTS, :], hf[:, u % 2, :], ACT.Copy).then_inc(h_hi_done, 1)

            def unit(f, u, it=0):
                silu_of(f, u, it)
                if 1 <= u < UNITS - 2:
                    g_split(f, u + 2, it)
                elif f == 2 and u == UNITS - 2:
                    g_split(None, 0)
                h_hi_of(f, u, it)
                if f == 0 and u == 0:
                    g_split(0, RAW_UNITS)
                if u + 1 < UNITS:
                    d_split(D0[f] + u + 1, it)

            def channel_major(e):
                for t in range(TT):
                    act.wait_ge(tr_done, 4 * e + 2 * t + 2)
                    bank = ps[:, WORK + 3, :].rearrange("p (k s) -> p k s", k=4)
                    if e == 0:
                        act.activation(xf[:, t, 4:8, :], bank, ACT.Copy).then_inc(xf_up_done, 4)
                    else:
                        for k in range(4, 8):
                            act.activation(xf[:, t, k, :], bank[:, k - 4, :], ACT.Identity, bias=lnT[:, 1, e, k:k + 1],
                                           scale=lnT[:, 0, e, k:k + 1]).then_inc(xf_up_done, 1)
                    if e == QKV_EVENT:
                        x_hi(e, t)
                if e != QKV_EVENT:
                    for t in range(TT):
                        x_hi(e, t)

            def x_hi(e, t):
                for q, ready in enumerate((xf_lo_done, xf_up_done)):
                    act.wait_ge(ready, 8 * e + 4 * t + 4)
                    act.activation(xT_hi[:, 4 * q:4 * q + 4, t * P:(t + 1) * P], xf[:, t, 4 * q:4 * q + 4, :], ACT.Copy).then_inc(x_hi_done, 1)

            act.dma_start(cst[:, 0, :], masks[0]).then_inc(ident_in, 16)
            act.dma_start(lnrow[:, 0, :], ln_g.rearrange("l n (k p) -> (l n k) p", p=P)).then_inc(small_in, 16)
            act.dma_start(lnrow[:, 1, :], ln_b.rearrange("l n (k p) -> (l n k) p", p=P)).then_inc(small_in, 16)
            act.dma_start(pos_i[:, :], positions[0].rearrange("(t p) -> p t", p=P), allow_slow_non_contiguous=True).then_inc(small_in, 16)
            act.dma_start(sinkb[:, :], sinks[0:1, :].to_broadcast([P, NQ])).then_inc(small_in, 16)
            act.dma_start(cst[:, 1:4, :], masks[1:4].rearrange("m p q -> p m q")).then_inc(cst_in, 16)
            act.wait_ge(consts, 1)
            act.activation(sm[:, 0, 0, 0:1], mhalf[:, :], ACT.Silu)
            channel_major(0)
            for f in range(FFNS):
                d_split(D0[f])
                for u in range(4):
                    unit(f, u)
                if f == 0:
                    act.wait_ge(ang_done, 1)
                    act.activation(rot[:, :, 1, :], ang[:, 0], ACT.Sin)
                    act.activation(rot[:, :, 0, :], ang[:, 1], ACT.Sin).then_inc(sin_done, 1)
                with act.Fori(0, (UNITS - 6) // 4) as it:
                    for u in range(4, 8):
                        unit(f, u, it)
                for u in range(UNITS - 2, UNITS):
                    unit(f, u)
                if f == 0:
                    for k in range(POOL_UNITS):
                        act.wait_ge(d_scaled, k + 1)
                        d_split(D_POOL + k)
                    for c in range(KT // 2):
                        act.wait_ge(u_done, c + 1)
                        for k in (2 * c, 2 * c + 1):
                            last = act.activation(xT_hi[:, k, :], ps[:, WORK + c, (k % 2) * S:(k % 2 + 1) * S], ACT.Copy, scale=lnT[:, 0, 0, k:k + 1])
                        last.then_inc(u_hi_done, 1)
                    g_split(1, RAW_UNITS)
                    channel_major(1)
                if f == 1:
                    g_split(2, RAW_UNITS)
                    channel_major(2)
                if f == 2:
                    g_split(None, 1)
                    channel_major(QKV_EVENT)
                    attention_act(act, g_split, d_split)
                    g_split(3, RAW_UNITS)
                    channel_major(4)

        def rotary_tables(dve, link):
            dve.wait_ge(small_in, 64)
            dve.wait_ge(consts, 1)
            turn, parts = 2.0 * math.pi, []
            for i in range(4):
                grid = 2.0 ** (9 + 11 * i)
                part = math.floor(turn * grid) / grid if i < 3 else float(np.float32(turn))
                parts.append(part)
                turn -= part
            A = [ang[:, i] for i in range(8)]
            magic = 1.5 * 2.0 ** 23
            link(dve.tensor_copy(ang[:, 7, :, 0], pos_i[:, :]))
            link(dve.tensor_tensor(A[0], ang[:, 7, :, 0:1].to_broadcast([P, TT, HALF]),
                                   invf[:, :].rearrange("p (a j) -> p a j", a=1).to_broadcast([P, TT, HALF]), ALU.mult))
            link(dve.tensor_scalar(A[2], A[0], 1.0 / (2.0 * math.pi), magic, ALU.mult, ALU.add))
            link(dve.tensor_scalar(A[2], A[2], magic, None, ALU.subtract))
            link(dve.tensor_scalar(A[3], A[2], 1.0 / 2048, magic, ALU.mult, ALU.add))
            link(dve.tensor_scalar(A[3], A[3], magic, 2048.0, ALU.subtract, ALU.mult))
            link(dve.tensor_tensor(A[2], A[2], A[3], ALU.subtract))
            for part in parts:
                for digit in (A[3], A[2]):
                    link(dve.scalar_tensor_tensor(A[0], digit, -part, A[0], ALU.mult, ALU.add))
            link(dve.tensor_scalar(A[1], A[0], math.pi / 2, None, ALU.add))
            link(dve.tensor_scalar(A[4], A[1], math.pi, -2.0 * math.pi, ALU.is_gt, ALU.mult))
            link(dve.tensor_tensor(A[1], A[1], A[4], ALU.add))
            top = 3.1415925
            link(dve.tensor_scalar(A[0], A[0], top, -top, ALU.min, ALU.max))
            dve.tensor_scalar(A[1], A[1], top, -top, ALU.min, ALU.max).then_inc(ang_done, 1)

        def attention_dve(dve, link, note, g_split, d_split):
            def rotate(v, tmp_a, tmp_b, heads, t):
                cos, sin, nsin = (rot[:, t, c, :].rearrange("p (a j) -> p a j", a=1).to_broadcast([P, heads, HALF]) for c in range(3))
                lo, hi = v[:, :, 0:HALF], v[:, :, HALF:ROT]
                dve.tensor_tensor(tmp_a[:, :, 0:HALF], lo, cos, ALU.mult)
                dve.tensor_tensor(tmp_a[:, :, HALF:ROT], hi, cos, ALU.mult)
                dve.tensor_tensor(tmp_b[:, :, 0:HALF], hi, nsin, ALU.mult)
                link(dve.tensor_tensor(tmp_b[:, :, HALF:ROT], lo, sin, ALU.mult))
                return dve.tensor_tensor(v[:, :, 0:ROT], tmp_a, tmp_b, ALU.add)

            def chunk(c, t):
                dve.wait_ge(qkv_done, 2 * c + t + 1)
                src = ps[:, (2 * c + t) % 4, :]
                if c == 0:
                    as_heads = lambda v: v.rearrange("p (g d) -> p g d", g=NKV)
                    dve.tensor_tensor(vd[:, t, :, 0, :], as_heads(src[:, 256:512]), as_heads(aux[:, 1280:1536]), ALU.add)
                    v, heads = kd[:, t, :, 0, :], NKV
                    link(dve.tensor_tensor(v, as_heads(src[:, 0:256]), as_heads(aux[:, 1024:1280]), ALU.add))
                else:
                    lo = 512 * (c - 1)
                    flat, heads = xn[:, t, lo:lo + 512], 8
                    v = flat.rearrange("p (h d) -> p h d", h=8)
                    if c == 1:
                        dve.wait_ge(ax_done, 8 + t + 1)
                    link(dve.tensor_tensor(flat, src, aux[:, lo:lo + 512], ALU.add))
                after(dve, qkv_sb, 2 * c + t)
                tmp = rtmp[:, :, 0:heads, :]
                rotate(v, tmp[:, 0], tmp[:, 1], heads, t).then_inc(qkv_sb, 1)

            def scores(i):
                g, n = TASKS[i]
                s = sc[i % 2]
                if n == 0:
                    dve.wait_ge(s_done, i + 1)
                    after(dve, pT_ps, i - 1)
                    ins = dve.tensor_tensor(s[:, :, :], ps[:, WORK, :].rearrange("p (h j) -> p h j", h=4),
                                            cst[:, 1:2, :].to_broadcast([P, 4, P]), ALU.add)
                else:
                    dve.wait_ge(diag_done, g + 1)
                    ins = dve.copy_predicated(s[:, :, :], cst[:, 2:3, :].bitcast(i32).to_broadcast([P, 4, P]), two_banks[:, :, 0:P])
                ins.then_inc(s_sb, 1)
                dve.wait_ge(s_sb, i + 1)
                st = sm[:, i % 2]
                sink = sinkb[:, 4 * g:4 * g + 4]
                link(dve.tensor_reduce(st[:, 0, :], s[:, :, :], axis=AX.X, op=ALU.max))
                link(dve.scalar_tensor_tensor(st[:, 5, :], st[:, 0, :], SCALE, sink, ALU.mult, ALU.max))
                dve.tensor_tensor(st[:, 2, :], sink, st[:, 5, :], ALU.subtract)
                dve.tensor_scalar(st[:, 1, :], st[:, 5, :], -1.0, None, ALU.mult).then_inc(m_done, 1)

            def probabilities(i):
                st = sm[:, i % 2]
                dve.wait_ge(e_done, i + 1)
                link(dve.tensor_tensor(st[:, 5, :], st[:, 3, :], st[:, 4, :], ALU.add))
                link(dve.reciprocal(st[:, 0, :], st[:, 5, :]))
                dve.tensor_tensor(sc[i % 2][:, :, :], sc[i % 2][:, :, :], st[:, 0, :].rearrange("p (h a) -> p h a", a=1).to_broadcast([P, 4, P]), ALU.mult).then_inc(p_done, 1)

            def pT_masked(i):
                if TASKS[i][1] == 1:
                    dve.wait_ge(pT_ps, i + 1)
                    src = ps[:, WORK + 2, :].rearrange("p (h q) -> p h q", h=4)
                    dve.tensor_tensor(pT[i % 2][:, 1], src, cst[:, 3:4, :].to_broadcast([P, 4, P]), ALU.mult)
                    dve.tensor_tensor(pT[i % 2][:, 0], src, prevT[:, :, :].to_broadcast([P, 4, P]), ALU.mult).then_inc(pT_v, 1)

            def o_lo(i):
                g, n = TASKS[i]
                dve.wait_ge(oT_hi_done, i + 1)
                bank = ps[:, WORK + 3, :].rearrange("p (a e q) -> p a e q", a=2, e=2)
                for e, rows in enumerate((slice(0, HD), slice(HD, P))):
                    last = dve.tensor_tensor(xT_lo[rows, 2 * g:2 * g + 2, n * P:(n + 1) * P], bank[rows, :, e, :],
                                             xT_hi[rows, 2 * g:2 * g + 2, n * P:(n + 1) * P].bitcast(f32), ALU.subtract)
                last.then_inc(oT_lo_done, 1)

            dve.wait_ge(sin_done, 1)
            link(dve.tensor_scalar(rot[:, :, 2, :], rot[:, :, 1, :], -1.0, None, ALU.mult))
            dve.wait_ge(aux_in, 64)
            dve.wait_ge(cst_in, 16)
            dve.wait_ge(x_lo_done, 4 * QKV_EVENT + 4)
            link(dve.tensor_scalar(prevT[:, 0, :], cst[:, 3, :], -1.0, 1.0, ALU.mult, ALU.add))
            chunk(0, 0)
            g_split(None, 2)
            chunk(0, 1)
            g_split(None, 3)
            d_split(D_WO)
            d_split(D_WO + 1)
            g_split(None, 4)
            chunk(1, 0)
            chunk(1, 1)
            g_split(None, 5)
            scores(0)
            for i in range(len(TASKS)):
                probabilities(i)
                if i >= 1:
                    o_lo(i - 1)
                pT_masked(i)
                if i + 1 < len(TASKS):
                    scores(i + 1)
                if i == 1:
                    chunk(2, 0)
                    chunk(2, 1)
                if i >= 2:
                    d_split(D_WO + i)
            o_lo(len(TASKS) - 1)


        @block.vector
        def _(dve):
            count = [0]

            def note(ins):
                count[0] += 1
                ins.then_inc(order, 1)
                return count[0]

            def link(ins):
                dve.wait_ge(order, note(ins))

            def g_split(f, u, it=0, halves=(0, 1)):
                X, G, src = split_unit(f, u)
                for half in halves:
                    dve.wait_ge(g_hi_done, 2 * X + half + 1 + 8 * it)
                    if halves == (1,):
                        dve.wait_ge(g_lo_done, 2 * X + 1)
                    dve.tensor_tensor(g_half(g_lo, X, half), src(G, half), g_half(g_hi, X, half).bitcast(f32), ALU.subtract).then_inc(g_lo_done, 1)

            def d_split(E, it=0):
                dve.wait_ge(d_hi_done, E + 1 + 4 * it)
                dve.tensor_tensor(d_lo[:, E % D_SLOTS, :], raw_d[:, (E // 2) % 2, E % 2, :], d_hi[:, E % D_SLOTS, :].bitcast(f32), ALU.subtract).then_inc(d_lo_done, 1)

            def h_of(f, u, it=0):
                dve.wait_ge(silu_done, UNITS * f + u + 1 + 4 * it)
                dve.tensor_tensor(hf[:, u % 2, :], silu[:, u % 2, :], ps[:, WORK + u % 2, S:2 * S], ALU.mult).then_inc(hf_done, 1)

            def h_lo_of(f, u, it=0):
                dve.wait_ge(h_hi_done, UNITS * f + u + 1 + 4 * it)
                slot = (D0[f] + u) % D_SLOTS
                dve.tensor_tensor(hT_lo[:, slot, :], hf[:, u % 2, :], hT_hi[:, slot, :].bitcast(f32), ALU.subtract).then_inc(h_lo_done, 1)

            def unit(f, u, it=0):
                h_of(f, u, it)
                if 1 <= u < UNITS - 2:
                    g_split(f, u + 2, it)
                elif f == 2 and u == UNITS - 2:
                    g_split(None, 0)
                h_lo_of(f, u, it)
                if f == 0 and u == 0:
                    g_split(0, RAW_UNITS)
                if u + 1 < UNITS:
                    d_split(D0[f] + u + 1, it)
                if f == 0 and u in (2, 3):
                    dve.tensor_scalar(ax[:, u - 2, :], xn[:, u - 2, :], ALPHA, None, ALU.mult).then_inc(ax_done, 1)
                elif u in (2, 3):
                    residual(FFN_EVENT[f], u - 2)

            HALVES = [slice(512 * h, 512 * (h + 1)) for h in range(2)]

            def statistics(n, t, coef, early=None):
                for h in range(2):
                    dve.wait_ge(acc_done, 4 * n + 2 * t + h + 1)
                    link(dve.scalar_tensor_tensor(xn[:, t, HALVES[h]], ACC[t][h], coef, ax[:, t, HALVES[h]], ALU.mult, ALU.add))
                    last = dve.bn_stats(stats[:, h, :], xn[:, t, HALVES[h]])
                    if h == 0:
                        note(last)
                        if early:
                            early()
                link(last)
                dve.bn_aggr(mv[:, t, :], stats[:, :, :].rearrange("p a b -> p (a b)")).then_inc(stat_done, 1)

            def normalise(n, t, coef, filler=None, early=None):
                statistics(n, t, coef, early)
                if filler:
                    filler(t)
                dve.wait_ge(rstd_done, 2 * n + t + 1)
                for h in range(2):
                    dve.tensor_scalar(xn[:, t, HALVES[h]], xn[:, t, HALVES[h]], mv[:, t, 0:1], rstd[:, t, 1:2],
                                      ALU.subtract, ALU.mult).then_inc(xn_done, 1)

            def normalise_out(n, t, coef):
                statistics(n, t, coef)
                if t == 0:
                    dve.wait_ge(gb_in, 32 * (n + 1))
                dve.wait_ge(stat_done, 2 * n + t + 1)
                for h in range(2):
                    dve.scalar_tensor_tensor(xn[:, t, HALVES[h]], xn[:, t, HALVES[h]], mv[:, t, 0:1], gb[:, 0, HALVES[h]],
                                             ALU.subtract, ALU.mult).then_inc(xn_done, 1)
                dve.wait_ge(rstd_done, 2 * n + t + 1)
                for h in range(2):
                    dve.wait_ge(xn_done, 4 * n + 2 * t + h + 1)
                    dve.scalar_tensor_tensor(xn[:, t, HALVES[h]], xn[:, t, HALVES[h]], rstd[:, t, 1:2], gb[:, 1, HALVES[h]],
                                             ALU.mult, ALU.add).then_inc(y_done, 1)

            def channel_major(e, t):
                dve.wait_ge(tr_done, 4 * e + 2 * t + 1)
                bank = ps[:, WORK + 2, :].rearrange("p (k s) -> p k s", k=4)
                if e == 0:
                    dve.tensor_copy(xf[:, t, 0:4, :], bank).then_inc(xf_lo_done, 4)
                else:
                    for k in range(4):
                        dve.tensor_scalar(xf[:, t, k, :], bank[:, k, :], lnT[:, 0, e, k:k + 1], lnT[:, 1, e, k:k + 1], ALU.mult, ALU.add).then_inc(xf_lo_done, 1)

            def x_lo(e, t):
                for q in range(2):
                    dve.wait_ge(x_hi_done, 4 * e + 2 * t + q + 1)
                    at = slice(4 * q, 4 * q + 4), slice(t * P, (t + 1) * P)
                    dve.tensor_tensor(xT_lo[:, at[0], at[1]], xf[:, t, at[0], :], xT_hi[:, at[0], at[1]].bitcast(f32),
                                      ALU.subtract).then_inc(x_lo_done, 1)

            def residual(n, t):
                if t == 0:
                    dve.wait_ge(gb_in, 32 * (n + 1))
                dve.wait_ge(xn_done, 4 * n + 2 * t + 2)
                link(dve.scalar_tensor_tensor(ax[:, t, :], xn[:, t, :], ALPHA, gb[:, 0, :], ALU.mult, ALU.mult))
                dve.scalar_tensor_tensor(ax[:, t, :], gb[:, 1, :], ALPHA, ax[:, t, :], ALU.mult, ALU.add).then_inc(ax_done, 1)

            for t in range(TT):
                channel_major(0, t)
            for t in range(TT):
                x_lo(0, t)
            for f in range(FFNS):
                d_split(D0[f])
                for u in range(4):
                    unit(f, u)
                    if f == 0 and u == 0:
                        dve.wait_ge(lnT_ps, 1)
                        dve.tensor_copy(lnT[:, :, :, :].rearrange("p a n k -> p (a n k)"), ps[:, 7, 0:96]).then_inc(lnT_done, 1)
                    if f == 0 and u == 2:
                        rotary_tables(dve, link)
                with dve.Fori(0, (UNITS - 6) // 4) as it:
                    for u in range(4, 8):
                        unit(f, u, it)
                for u in range(UNITS - 2, UNITS):
                    unit(f, u)
                if f == 0:
                    for t in range(TT):
                        normalise(0, t, 0.5, filler=lambda t: d_split(D_POOL + t))
                    for c in range(KT // 2):
                        dve.wait_ge(u_hi_done, c + 1)
                        for k in (2 * c, 2 * c + 1):
                            last = dve.scalar_tensor_tensor(xT_lo[:, k, :], ps[:, WORK + c, (k % 2) * S:(k % 2 + 1) * S], lnT[:, 0, 0, k:k + 1],
                                                            xT_hi[:, k, :].bitcast(f32), ALU.mult, ALU.subtract)
                        last.then_inc(u_lo_done, 1)
                    for t in range(TT):
                        dve.wait_ge(ax_done, 2 + t + 1)
                        normalise(1, t, 1.0, filler=lambda t: g_split(1, RAW_UNITS, halves=(t,)))
                        channel_major(1, t)
                    for t in range(TT):
                        x_lo(1, t)
                elif f == 1:
                    for t in range(TT):
                        normalise(2, t, 0.5, filler=lambda t: g_split(2, RAW_UNITS, halves=(t,)))
                        channel_major(2, t)
                    for t in range(TT):
                        x_lo(2, t)
                elif f == 2:
                    normalise(3, 0, 0.5, filler=lambda t: g_split(None, 1, halves=(1,)))
                    channel_major(QKV_EVENT, 0)
                    normalise(3, 1, 0.5, early=lambda: x_lo(QKV_EVENT, 0))
                    channel_major(QKV_EVENT, 1)
                    x_lo(QKV_EVENT, 1)
                    attention_dve(dve, link, note, g_split, d_split)
                    for t in range(TT):
                        dve.wait_ge(ax_done, 8 + t + 1)
                        normalise(4, t, 1.0, filler=lambda t: g_split(3, RAW_UNITS, halves=(t,)))
                        channel_major(4, t)
                    for t in range(TT):
                        x_lo(4, t)
                else:
                    for t in range(TT):
                        normalise_out(5, t, 0.5)

        def pool_pe(pe, three):
            pe.wait_ge(band_in, 16)
            pe.wait_ge(hf_done, UNITS)
            for t in range(TT):
                for c in range(KT // 2):
                    for k in (2 * c, 2 * c + 1):
                        b = band[:, k // 2, :]
                        o = ps[:, WORK + c, (k % 2) * S:(k % 2 + 1) * S]
                        if k % 4 == 0:
                            pe.wait_ge(xn_done, 2 * t + k // 4 + 1)
                        if t == 0:
                            last = pe.matmul(o, xn[:, 0, k * P:(k + 1) * P], b[:, 0:S], start=k % 2 == 0, stop=False)
                            if k == 0:
                                last.then_inc(d_used, 1)
                        else:
                            last = pe.matmul(o[:, P:S], xn[:, 1, k * P:(k + 1) * P], b[:, S:S + P], start=False, stop=k % 2 == 1)
                    if t == 1:
                        last.then_inc(u_done, 1)
            for t in range(TT):
                for g in range(len(WINDOWS)):
                    for j in range(2):
                        k, E = 2 * g + j, D_POOL + j
                        if t == 0:
                            pe.wait_ge(u_lo_done, g + 1)
                            if g == 0:
                                pe.wait_ge(d_lo_done, E + 1)
                        tok = slice(t * P, (t + 1) * P)
                        w_hi, w_lo = (b[:, E % D_SLOTS, g * GC:(g + 1) * GC] for b in (d_hi, d_lo))
                        last = three(ACC[t][g // 2][:, (g % 2) * GC:(g % 2 + 1) * GC], xT_hi[:, k, tok], xT_lo[:, k, tok],
                                     w_hi, w_lo, j == 0, j == 1)
                    if g % 2 == 1:
                        last.then_inc(acc_done, 1)

        def attention_pe(pe, three, down, transposes, rest_of_ffn):
            ident = cst[:, 0, :]
            e = QKV_EVENT

            def qkv(c, half, t, used=False, part=None, d_counted=False):
                X = X_QKV + 2 * c + half
                bank = ps[:, (2 * c + t) % 4, :]
                tok = slice(t * P, (t + 1) * P)
                if part != 1:
                    if c == 0:
                        pe.wait_ge(x_hi_done, 4 * e + 2 * t + half + 1)
                    if c == 2 and half == 0:
                        pe.wait_ge(qkv_sb, t + 1)
                    for j in range(4):
                        if t == 0 and j % 2 == 0:
                            pe.wait_ge(g_lo_done, 2 * X + j // 2 + 1)
                        w_hi, w_lo = (b[:, X % G_SLOTS, 512 * j:512 * (j + 1)] for b in (g_hi, g_lo))
                        k = 4 * half + j
                        ins = pe.matmul(bank, xT_hi[:, k, tok], w_hi, start=k == 0, stop=False)
                        if j == 0 and (used or d_counted):
                            ins.then_inc(d_used if d_counted else g_used, 1)
                        pe.matmul(bank, xT_hi[:, k, tok], w_lo, start=False, stop=False)
                if part != 0:
                    if c == 0:
                        pe.wait_ge(x_lo_done, 4 * e + 2 * t + half + 1)
                    for j in range(4):
                        k = 4 * half + j
                        last = pe.matmul(bank, xT_lo[:, k, tok], g_hi[:, X % G_SLOTS, 512 * j:512 * (j + 1)], start=False, stop=k == KT - 1)
                    return last

            def to_channels(c, t, used=False):
                if c == 0:
                    pe.wait_ge(dup_done, t + 1)
                    pe.wait_ge((xf_lo_done, xf_up_done)[t], 8 * e + 8)
                else:
                    pe.wait_ge(qkv_sb, 2 * c + t + 1)
                    if c == 1:
                        pe.wait_ge(qkT_done, t + 1)
                for j in range(4):
                    src = kd[:, t, j, :, :].rearrange("p e d -> p (e d)") if c == 0 else xn[:, t, 512 * (c - 1) + P * j:512 * (c - 1) + P * (j + 1)]
                    last = pe.transpose(ps[:, (2 if c == 2 else WORK + 2) + t, P * j:P * (j + 1)], src, ident)
                    if j == 0 and used:
                        last.then_inc(g_used, 1)
                last.then_inc(qkT_ps, 1)

            def scores(i):
                g, n = TASKS[i]
                if i == 0:
                    pe.wait_ge(hf_done, 3 * UNITS)
                if i in (0, 1, 4):
                    pe.wait_ge(qkT_done, {0: 3, 1: 4, 4: 6}[i])
                after(pe, s_sb, i)
                for h in range(4):
                    head = 4 * g + h
                    keys = slice(0, (n + 1) * P)
                    o = ps[:, WORK, P * h:P * (h + 1)] if n == 0 else two_banks[:, h, :]
                    last = pe.matmul(o, qT[:, head // 2, n * P:(n + 1) * P], kT[:, g, head % 2, keys], start=True, stop=True)
                last.then_inc(s_done, 1)

            def probs_T(i):
                if i == 0:
                    pe.wait_ge(qkT_done, 3)
                pe.wait_ge(p_done, i + 1)
                for h in range(4):
                    last = pe.transpose(ps[:, WORK + 2, P * h:P * (h + 1)], sc[i % 2][:, h, :], ident)
                last.then_inc(pT_ps, 1)

            def values(i):
                g, n = TASKS[i]
                pe.wait_ge(pT_a if n == 0 else pT_v, g + 1)
                after(pe, oT_lo_done, i)
                o = ps[:, WORK + 3, :]
                own = pT[i % 2][:, 1].rearrange("p h q -> p (h q)")
                prev = pT[i % 2][:, 0].rearrange("p h q -> p (h q)")
                v = [vd[:, t, g, :, :].rearrange("p e d -> p (e d)") for t in range(TT)]
                if i == 0:
                    pe.wait_ge(qkT_done, 4)
                if n == 1:
                    ins = pe.matmul(o, v[0], prev, start=True, stop=False)
                    if i == 1:
                        ins.then_inc(g_used, 1)
                pe.matmul(o, v[n], own, start=n == 0, stop=True).then_inc(oT_ps, 1)

            def wo(k, ts=(0, 1)):
                if ts[0] == 0:
                    pe.wait_ge(oT_lo_done, 2 * (k // 2) + (2 if ts[-1] == 1 else 1))
                    if k == 0:
                        pe.wait_ge(qkT_done, 6)
                else:
                    pe.wait_ge(oT_lo_done, 2 * (k // 2) + 2)
                down(D_WO + k, xT_hi[:, k, :], xT_lo[:, k, :], ts, k == 0, k == WO_UNITS - 1)

            transposes(e, 0)
            rest_of_ffn()
            qkv(0, 0, 0, d_counted=True)
            qkv(0, 1, 0, part=0)
            transposes(e, 1)
            qkv(0, 1, 0, part=1).then_inc(qkv_done, 1)
            qkv(0, 0, 1).then_inc(g_used, 1)
            qkv(0, 1, 1).then_inc(qkv_done, 1)
            qkv(1, 0, 0, used=True)
            qkv(1, 0, 1).then_inc(g_used, 1)
            qkv(1, 1, 0).then_inc(qkv_done, 1)
            to_channels(0, 0)
            qkv(1, 1, 1).then_inc(qkv_done, 1)
            to_channels(0, 1, used=True)
            to_channels(1, 0)
            qkv(2, 0, 0)
            scores(0)
            to_channels(1, 1)
            qkv(2, 0, 1).then_inc(g_used, 1)
            for i in range(len(TASKS)):
                if i + 1 < len(TASKS):
                    scores(i + 1)
                if i == 2:
                    to_channels(2, 0)
                    to_channels(2, 1)
                if i == 7:
                    wo(5, (0,))
                probs_T(i)
                if i < 2:
                    qkv(2, 1, i).then_inc(qkv_done, 1)
                elif i < 7:
                    wo(i - 2, (0, 1) if i < 6 else (0,))
                else:
                    wo(4, (1,))
                values(i)
            wo(6, (0,))
            wo(7, (0,))
            for k in range(5, 8):
                wo(k, (1,))

        @block.tensor
        def _(pe):
            ident = cst[:, 0, :]

            def three(out_, l_hi, l_lo, r_hi, r_lo, start, stop):
                pe.matmul(out_, l_hi, r_hi, start=start, stop=False)
                pe.matmul(out_, l_hi, r_lo, start=False, stop=False)
                return pe.matmul(out_, l_lo, r_hi, start=False, stop=stop)

            def gate_up_raw(f, u, t, ms=(0, 1)):
                e, G = FFN_EVENT[f], G0[f] + u
                if f > 0 and u == 0 and t == 0 or f == 0 and u == 1 and t == 0 and ms[0] == 0:
                    pe.wait_ge(g_in[(G // 2) % 2], 32 * (G // 4 + 1))
                for m in ms:
                    if f == 0 and u == 0 and t == 0:
                        pe.wait_ge(unit0_in[m], 16)
                    for i, k in enumerate((0, 4, 1, 5, 2, 6, 3, 7) if f > 0 else range(KT)):
                        if m == 0 and u == 0:
                            pe.wait_ge((xf_lo_done, xf_up_done)[k // 4], 8 * e + 4 * t + k % 4 + 1)
                        last = pe.matmul(ps[:, WORK + u % 2, m * S + t * P:m * S + (t + 1) * P], raw_unit(G, m)[:, k, :],
                                         xf[:, t, k, :], start=i == 0, stop=i == KT - 1)
                if t == TT - 1:
                    last.then_inc(g_used, 1)

            def gate_up(f, u, it=0):
                X = X0[f] + u
                pe.wait_ge(g_lo_done, 2 * X + 2 + 8 * it)
                pe.wait_ge(hf_done, UNITS * f + u - 1 + 4 * it)
                for m in range(2):
                    for k in range(KT):
                        if u == RAW_UNITS and m == 0 and k == 0:
                            pe.wait_ge(x_lo_done, 4 * FFN_EVENT[f] + 4)
                        w_hi, w_lo = g_half(g_hi, X, m)[:, k, :], g_half(g_lo, X, m)[:, k, :]
                        last = three(ps[:, WORK + u % 2, m * S:(m + 1) * S], w_hi, w_lo,
                                     xT_hi[:, k, :], xT_lo[:, k, :], k == 0, k == KT - 1)
                last.then_inc(g_used, 1)

            def down(E, l_hi, l_lo, ts, first, final, it=0):
                if ts[0] == 0:
                    pe.wait_ge(d_lo_done, E + 1 + 4 * it)
                for t in ts:
                    for h in range(2):
                        w_hi, w_lo = (b[:, E % D_SLOTS, 512 * h:512 * (h + 1)] for b in (d_hi, d_lo))
                        tok = slice(t * P, (t + 1) * P)
                        last = three(ACC[t][h], l_hi[:, tok], l_lo[:, tok], w_hi, w_lo, first, final)
                        if final:
                            last.then_inc(acc_done, 1)
                if not final and ts[-1] == TT - 1:
                    last.then_inc(d_used, 1)

            def ffn_down(f, u, ts=(0, 1), it=0):
                if ts[0] == 0:
                    pe.wait_ge(h_lo_done, UNITS * f + u + 1 + 4 * it)
                E = D0[f] + u
                final = u == UNITS - 1
                down(E, hT_hi[:, E % D_SLOTS, :], hT_lo[:, E % D_SLOTS, :], ts, u == 0, final, it)

            def transposes(e, t, used=0):
                if e == 1:
                    pe.wait_ge(lnT_done, 1)
                for q in range(2):
                    pe.wait_ge(*((xn_done, 4 * e + 2 * t + q + 1) if e > 0 else (x_in[t], 16)))
                    after(pe, (xf_lo_done, xf_up_done)[q], 8 * e + 4 * t)
                    for k in range(4 * q, 4 * q + 4):
                        last = pe.transpose(ps[:, WORK + 2 + q, (k % 4) * P:(k % 4 + 1) * P], xn[:, t, k * P:(k + 1) * P], ident)
                        if k == 0 and used:
                            last.then_inc(d_used, used)
                    last.then_inc(tr_done, 1)

            pe.wait_ge(ident_in, 16)
            for f in range(FFNS):
                e = FFN_EVENT[f]
                transposes(e, 0, used=(0, 2, 1, 1)[f])
                gate_up_raw(f, 0, 0)
                gate_up_raw(f, 1, 0, (0,))
                transposes(e, 1)
                gate_up_raw(f, 1, 0, (1,))
                gate_up_raw(f, 0, 1)
                gate_up_raw(f, 1, 1)
                if f == 0:
                    pe.wait_ge(small_in, 64)
                    pe.wait_ge(xf_up_done, 8)
                    for a in range(2):
                        last = pe.transpose(ps[:, 7, 48 * a:48 * (a + 1)], lnrow[:, a, :], ident[0:48, 0:48])
                    last.then_inc(lnT_ps, 1)
                ffn_down(f, 0)
                with pe.Fori(0, (UNITS - 6) // 4) as it:
                    for u in range(2, 6):
                        gate_up(f, u, it)
                        ffn_down(f, u - 1, it=it)
                last_u = UNITS - 4
                gate_up(f, last_u)
                ffn_down(f, last_u - 1)
                gate_up(f, last_u + 1)
                ffn_down(f, last_u, (0,))
                gate_up(f, last_u + 2)
                ffn_down(f, last_u + 1, (0,))
                gate_up(f, last_u + 3)
                ffn_down(f, last_u + 2, (0,))
                ffn_down(f, last_u, (1,))
                ffn_down(f, last_u + 3, (0,))
                ffn_down(f, last_u + 1, (1,))
                ffn_down(f, last_u + 2, (1,))
                if f != 2:
                    ffn_down(f, last_u + 3, (1,))
                if f == 0:
                    pool_pe(pe, three)
                if f == 2:
                    attention_pe(pe, three, down, transposes, lambda: ffn_down(2, UNITS - 1, (1,)))

_INS = ["x", "positions", "ln_g", "ln_b", "ffn_w_gate", "ffn_w_up", "ffn_w_down", "pool_w", "pool_b", "pool_scale",
        "attn_w_qkv", "attn_b_qkv", "attn_sinks", "attn_w_o", "attn_b_o"]


def pool_bands():
    full = np.zeros((4, S, S), np.float64)
    for g, win in enumerate(WINDOWS):
        for s in range(S):
            lo = max(s + 1 - win, 0)
            full[g, lo:s + 1, s] = 1.0 / (s + 1 - lo)
            full[g, s, s] -= 1.0
    return np.concatenate([full[:, :P, :], full[:, P:, P:]], axis=2).astype(np.float32)


def attention_masks():
    q, j = np.arange(P)[:, None], np.arange(P)[None, :]
    eye = (q == j)
    return np.stack([eye, (j > q) * NEG, j > q, j >= q]).astype(np.float32)


def kernel(**inputs):
    import concourse.bacc as bacc
    from concourse.bass_utils import run_bass_kernel_spmd

    nc = bacc.Bacc("TRN2", target_bir_lowering=False, num_devices=1)
    arrays, args = {}, []
    named = [(n, inputs[n]) for n in _INS] + [("bands", pool_bands()), ("masks", attention_masks())]
    for name, a in named:
        a = np.ascontiguousarray(a)
        arrays[f"in_{name}"] = a
        args.append(nc.dram_tensor(f"in_{name}", a.shape, mybir.dt.from_np(a.dtype), kind="ExternalInput").ap())
    args.append(nc.dram_tensor("out_y", (1, S, D), mybir.dt.float32, kind="ExternalOutput").ap())
    trunk_kernel(nc, *args)
    r = run_bass_kernel_spmd(nc, [arrays], core_ids=[0])
    return r.results[0]["out_y"]
```
